# Optimizing a Trainium2 kernel written in Bass

```python
import math
import jax, jax.numpy as jnp
from jax import lax
import numpy as np

D_MODEL = 1024
BATCH = 1
SEQ = 256
DEPTH = 2

HEAD_DIM = 64
N_HEADS = D_MODEL // HEAD_DIM
H_DSA = N_HEADS // 2
H_FOX = N_HEADS - H_DSA
D_LATENT = D_MODEL // 8
H_IDX = 8
D_IDX = 64
TOPK_MAX = 256
Q_BLOCK = 128
D_FF = ((8 * D_MODEL // 3 + 127) // 128) * 128
N_BUCKETS = 32
MAX_DISTANCE = 128
EPS = 1e-6
NEG = -1e30

kernel_name = 'hybrid_dsa_fox_macaron'

def rms_norm(x, g):
    xf = x.astype(jnp.float32)
    y = xf * lax.rsqrt(jnp.mean(xf * xf, axis=-1, keepdims=True) + EPS)
    return (y * g.astype(jnp.float32)).astype(x.dtype)

def swiglu(x, w_gate, w_up, w_down):
    return (jax.nn.silu(x @ w_gate) * (x @ w_up)) @ w_down

def t5_bucket(dist):
    n = jnp.maximum(dist, 0)
    max_exact = N_BUCKETS // 2
    nf = jnp.maximum(n, 1).astype(jnp.float32)
    large = max_exact + (jnp.log(nf / max_exact) / math.log(MAX_DISTANCE / max_exact)
                         * (N_BUCKETS - max_exact)).astype(jnp.int32)
    large = jnp.minimum(large, N_BUCKETS - 1)
    return jnp.where(n < max_exact, n, large)

def to_blocks(a):
    b, s = a.shape[:2]
    return jnp.moveaxis(a.reshape((b, s // Q_BLOCK, Q_BLOCK) + a.shape[2:]), 1, 0)

def from_blocks(a):
    nb, b, qb = a.shape[:3]
    return jnp.moveaxis(a, 0, 1).reshape((b, nb * qb) + a.shape[3:])

def dsa_attention(q, c_kv, q_idx, k_idx, w_idx, w_uk, w_uv, rel_bias):
    b, s = q.shape[:2]
    k_sel = min(TOPK_MAX, s // 4)
    q_lat = jnp.einsum('bshd,chd->bshc', q, w_uk)
    key_pos = jnp.arange(s)

    def block(args):
        blk, ql, qi, wi = args
        t = blk * Q_BLOCK + jnp.arange(Q_BLOCK)
        rel = jnp.einsum('bqhd,bsd->bqhs', qi, k_idx).astype(jnp.float32) * (D_IDX ** -0.5)
        score = jnp.einsum('bqh,bqhs->bqs', wi.astype(jnp.float32) * (H_IDX ** -0.5), jax.nn.relu(rel))
        score = jnp.where(key_pos[None, None, :] <= t[None, :, None], score, NEG)
        _, idx = lax.top_k(score, k_sel)
        c_sel = jax.vmap(lambda cb, ib: cb[ib])(c_kv, idx)
        dist = t[None, :, None] - idx
        bias = jnp.moveaxis(rel_bias[t5_bucket(dist)], -1, 2)
        logits = (jnp.einsum('bqhc,bqkc->bqhk', ql, c_sel).astype(jnp.float32) * (HEAD_DIM ** -0.5)
                  + bias.astype(jnp.float32))
        logits = jnp.where((dist >= 0)[:, :, None, :], logits, NEG)
        p = jax.nn.softmax(logits, axis=-1).astype(c_kv.dtype)
        return jnp.einsum('bqhk,bqkc->bqhc', p, c_sel)

    nb = s // Q_BLOCK
    o_lat = from_blocks(lax.map(block, (jnp.arange(nb), to_blocks(q_lat), to_blocks(q_idx), to_blocks(w_idx))))
    return jnp.einsum('bshc,chd->bshd', o_lat, w_uv)

def fox_attention(q, k, v, log_f):
    b, s = q.shape[:2]
    cum = jnp.cumsum(log_f, axis=1)
    cum_k = jnp.moveaxis(cum, 1, 2)
    key_pos = jnp.arange(s)

    def block(args):
        blk, qb, cq = args
        t = blk * Q_BLOCK + jnp.arange(Q_BLOCK)
        logits = (jnp.einsum('bqhd,bshd->bhqs', qb, k).astype(jnp.float32) * (HEAD_DIM ** -0.5)
                  + jnp.moveaxis(cq, 1, 2)[..., None] - cum_k[:, :, None, :])
        logits = jnp.where(key_pos[None, None, None, :] <= t[None, None, :, None], logits, NEG)
        p = jax.nn.softmax(logits, axis=-1).astype(v.dtype)
        return jnp.einsum('bhqs,bshd->bqhd', p, v)

    nb = s // Q_BLOCK
    return from_blocks(lax.map(block, (jnp.arange(nb), to_blocks(q), to_blocks(cum))))

def token_mixing(h, w_in, b_forget, g_ckv, w_uk, w_uv, w_out, rel_bias):
    b, s, _ = h.shape
    sizes = [H_DSA * HEAD_DIM, D_LATENT, H_IDX * D_IDX, D_IDX, H_IDX, 3 * H_FOX * HEAD_DIM, H_FOX]
    points = []
    acc = 0
    for sz in sizes[:-1]:
        acc += sz
        points.append(acc)
    proj = h @ w_in
    q_a, c_raw, q_i, k_i, w_i, qkv_f, f_logit = jnp.split(proj, points, axis=-1)
    q_a = q_a.reshape(b, s, H_DSA, HEAD_DIM)
    c_kv = rms_norm(c_raw, g_ckv)
    q_i = q_i.reshape(b, s, H_IDX, D_IDX)
    qkv_f = qkv_f.reshape(b, s, 3, H_FOX, HEAD_DIM)
    log_f = jax.nn.log_sigmoid(f_logit.astype(jnp.float32) + b_forget.astype(jnp.float32))
    o_a = dsa_attention(q_a, c_kv, q_i, k_i, w_i, w_uk, w_uv, rel_bias)
    o_f = fox_attention(qkv_f[:, :, 0], qkv_f[:, :, 1], qkv_f[:, :, 2], log_f)
    o = jnp.concatenate([o_a.reshape(b, s, H_DSA * HEAD_DIM), o_f.reshape(b, s, H_FOX * HEAD_DIM)], axis=-1)
    return o @ w_out

def setup_inputs(seed: int = 0) -> dict:
    key = jax.random.key(seed)
    ks = jax.random.split(key, 20)
    in_width = H_DSA * HEAD_DIM + D_LATENT + H_IDX * D_IDX + D_IDX + H_IDX + 3 * H_FOX * HEAD_DIM + H_FOX
    f32 = jnp.float32

    def nrm(k, shape, fan_in):
        return jax.random.normal(k, shape, f32) * (fan_in ** -0.5)

    def gain(k, shape):
        return 1.0 + 0.05 * jax.random.normal(k, shape, f32)

    return {
        'x': jax.random.normal(ks[0], (BATCH, SEQ, D_MODEL), f32),
        'ffn1_norm': gain(ks[1], (DEPTH, D_MODEL)),
        'ffn1_gate': nrm(ks[2], (DEPTH, D_MODEL, D_FF), D_MODEL),
        'ffn1_up': nrm(ks[3], (DEPTH, D_MODEL, D_FF), D_MODEL),
        'ffn1_down': nrm(ks[4], (DEPTH, D_FF, D_MODEL), D_FF),
        'mix_norm': gain(ks[5], (DEPTH, D_MODEL)),
        'w_in': nrm(ks[6], (DEPTH, D_MODEL, in_width), D_MODEL),
        'b_forget': 2.0 + 3.0 * jax.random.uniform(ks[7], (DEPTH, H_FOX), f32),
        'ckv_norm': gain(ks[8], (DEPTH, D_LATENT)),
        'w_uk': nrm(ks[9], (DEPTH, D_LATENT, H_DSA, HEAD_DIM), D_LATENT),
        'w_uv': nrm(ks[10], (DEPTH, D_LATENT, H_DSA, HEAD_DIM), D_LATENT),
        'w_out': nrm(ks[11], (DEPTH, D_MODEL, D_MODEL), D_MODEL),
        'ffn2_norm': gain(ks[12], (DEPTH, D_MODEL)),
        'ffn2_gate': nrm(ks[13], (DEPTH, D_MODEL, D_FF), D_MODEL),
        'ffn2_up': nrm(ks[14], (DEPTH, D_MODEL, D_FF), D_MODEL),
        'ffn2_down': nrm(ks[15], (DEPTH, D_FF, D_MODEL), D_FF),
        'rel_bias': 0.5 * jax.random.normal(ks[16], (N_BUCKETS, H_DSA), f32),
        'final_norm': gain(ks[17], (D_MODEL,)),
    }

def reference(x, ffn1_norm, ffn1_gate, ffn1_up, ffn1_down, mix_norm, w_in, b_forget, ckv_norm,
              w_uk, w_uv, w_out, ffn2_norm, ffn2_gate, ffn2_up, ffn2_down, rel_bias, final_norm):
    h = x
    for l in range(DEPTH):
        h = h + 0.5 * swiglu(rms_norm(h, ffn1_norm[l]), ffn1_gate[l], ffn1_up[l], ffn1_down[l])
        h = h + token_mixing(rms_norm(h, mix_norm[l]), w_in[l], b_forget[l], ckv_norm[l],
                             w_uk[l], w_uv[l], w_out[l], rel_bias)
        h = h + 0.5 * swiglu(rms_norm(h, ffn2_norm[l]), ffn2_gate[l], ffn2_up[l], ffn2_down[l])
    return rms_norm(h, final_norm)


_drawn_inputs = setup_inputs


def setup_inputs(seed=0):
    import zlib

    import numpy as np

    out = dict(_drawn_inputs(seed))
    spreads = {}
    factors = {}
    for name, (base, spread) in spreads.items():
        noise = np.random.default_rng([zlib.crc32(name.encode()), seed]).standard_normal(out[name].shape)
        drawn = base * np.exp(spread * noise) if base else spread * noise
        out[name] = __import__('jax').numpy.asarray(drawn.astype(out[name].dtype))
    for name, factor in factors.items():
        out[name] = (out[name] * factor).astype(out[name].dtype)
    return out
```

```python
from contextlib import ExitStack

import numpy as np

import concourse.bass as bass
from concourse import mybir

F32 = mybir.dt.float32
F32R = mybir.dt.float32r
BF16 = mybir.dt.bfloat16
ALU = mybir.AluOpType
ACT = mybir.ActivationFunctionType

P = 128
D = 1024
S = 256
S3 = 3 * P
DEPTH = 2
NB = S // P
KT = D // P
HD = 64
NH = 8
TOPK = S // 4
DFF = ((8 * D // 3 + P - 1) // P) * P
NF = DFF // P
NBUCKET = 32
MAXDIST = 128
EPS = 1e-6
NEG = -1e30
TAKEN = -3e38
LOWEST = -3.4e38
SCALE = HD ** -0.5
W_SCALE = NH ** -0.5

UNIT = 1024
FRONT = 2 * UNIT
CHUNK = 3 * UNIT
MIXC = 12
LC = 2 * NF + MIXC
NCHUNK = DEPTH * LC
TAB = 384
TINY = 8

MIX_USED = [(UNIT + P, UNIT), (FRONT, UNIT), (FRONT, UNIT), (FRONT, UNIT), (FRONT, UNIT), (FRONT, UNIT),
            (FRONT, TINY), (FRONT, UNIT), (UNIT, TINY), (FRONT, UNIT), (FRONT, UNIT), (FRONT, TINY)]

KI, QI, KA, QA, FX = 0, 1, 5, 9, 13
NFEAT = 21

G_FFN1, G_MIX, G_FFN2, G_CKV, G_BF = 0, KT, 2 * KT, 3 * KT, 3 * KT + 1
NG = G_BF + NH
C_ID = 0
C_CM = C_ID + P
C_NC = C_CM + S
C_U = C_NC + S3
C_E = C_U + NB * S
C_OH = C_E + NH * P
C_RB = C_OH + TAB
NC = C_RB + NH


def trunk(nc, x, stream, gains, final_gain, consts, rel_bias, out, table):
    with ExitStack() as ctx:
        def sb(name, shape, dt=F32):
            return ctx.enter_context(nc.sbuf_tensor(name, shape, dt))

        def sems(names):
            return [ctx.enter_context(nc.semaphore(n)) for n in names.split()]

        raw = sb("raw", [P, 2, CHUNK])
        whi = sb("whi", [P, 2, CHUNK], F32R)
        wlo = sb("wlo", [P, 2, CHUNK], F32R)
        X = sb("X", [P, NB, D])
        xn = sb("xn", [P, NB, D])
        xhi = sb("xhi", [P, KT, S], F32R)
        xlo = sb("xlo", [P, KT, S], F32R)
        junk = sb("junk", [P, NB, D])
        rbb = sb("rbb", [NBUCKET, NH, P])
        ss = sb("ss", [P, NB])
        ms = sb("ms", [P, NB])
        rstd = sb("rstd", [P, NB])
        mhalf = sb("mhalf", [P, NB])
        gains_all = sb("gains_all", [P, DEPTH, NG])
        gain = sb("gain", [P, NG])
        fgain = sb("fgain", [P, D])
        sig = sb("sig", [P, 2, S])
        hg = sb("hg", [P, 2, S])
        hf = sb("hf", [P, 2, S])
        hhi = sb("hhi", [P, 2, S], F32R)
        hlo = sb("hlo", [P, 2, S], F32R)
        cst = sb("cst", [P, NC])
        nident = sb("nident", [P, P], BF16)
        bias = sb("bias", [P, NH, S])
        feat = sb("feat", [P, NFEAT, S])
        val = sb("val", [P, NB, D])
        wf = sb("wf", [P, NB, NH])
        zf = sb("zf", [P, NB, NH])
        az = sb("az", [P, NB, NH])
        mz = sb("mz", [P, NB, NH])
        ez = sb("ez", [P, NB, NH])
        lz = sb("lz", [P, NB, NH])
        logf = sb("logf", [P, NB, NH])
        ncum = sb("ncum", [NH, S3])
        cumq = sb("cumq", [P, NB, NH])
        css = sb("css", [P, NB])
        cms = sb("cms", [P, NB])
        crstd = sb("crstd", [P, NB])
        cn = sb("cn", [P, NB, P])
        chi = sb("chi", [P, S], F32R)
        clo = sb("clo", [P, S], F32R)
        relu = sb("relu", [P, 2, S3])
        score = sb("score", [P, S3])
        top8 = sb("top8", [P, 8])
        drop = sb("drop", [P, S3], BF16)
        lg = sb("lg", [P, 2, S3])
        mx = sb("mx", [P, 2, NB])
        mt = sb("mt", [P, 2, NB])
        nm = sb("nm", [P, 2, NB])
        pr = sb("pr", [P, 2, S3])
        prT = sb("prT", [P, 2, S3])
        rsum = sb("rsum", [P, NB, 2 * NH])
        rinv = sb("rinv", [P, NB, 2 * NH])
        spare = sb("spare", [P, 1])

        ident = cst[:, C_ID:C_ID + P]
        cmask = cst[:, C_CM:C_CM + S]
        noncausal = cst[:, C_NC:C_NC + S3]
        tri = cst[:, C_U:C_U + NB * S].rearrange("p (b t) -> p b t", b=NB)
        pick = cst[0:NH, C_E:C_E + NH * P].rearrange("p (h q) -> p h q", h=NH)
        onehot = cst[0:NBUCKET, C_OH:C_OH + TAB]
        rb = cst[0:NBUCKET, C_RB:C_RB + NH]
        tab = feat[:, 0:12, :].rearrange("p a t -> p (a t)").rearrange("p (h y) -> p h y", h=NH)

        ps = ctx.enter_context(nc.psum_tensor("ps", [P, 8, 512], F32))
        GU = 4
        WFB, CB = 3, 2
        CUMT, CUMQ = 64, 64 + S

        raw_in = sems("raw_in0 raw_in1")
        x_in, const_in, rb_in, gain_in, fgain_in = sems("x_in const_in rb_in gain_in fgain_in")
        table_out, bias_in, out_done = sems("table_out bias_in out_done")
        half_set, nident_set, rbb_set, gain_set, tab_mm, tab_sb = sems(
            "half_set nident_set rbb_set gain_set tab_mm tab_sb")
        hi_front, hi_back = sems("hi_front hi_back")
        w_front, w_back = sems("w_front w_back")
        front_done, back_done = sems("front_done back_done")
        x_ready, ss_out, ms_out, rstd_out, xn_out = sems("x_ready ss_out ms_out rstd_out xn_out")
        xt_mm, xhi_out, xlo_out = sems("xt_mm xhi_out xlo_out")
        sig_out, hg_out, h_out, hhi_out, hlo_out, acc_mm = sems("sig_out hg_out h_out hhi_out hlo_out acc_mm")
        feat_mm, feat_out, wf_mm, wo_mm = sems("feat_mm feat_out wf_mm wo_mm")
        z_out, az_out, ez_out, lz_out, logf_out = sems("z_out az_out ez_out lz_out logf_out")
        cum_mm, cum_out = sems("cum_mm cum_out")
        c_mm, css_out, cms_out, crstd_out = sems("c_mm css_out cms_out crstd_out")
        cn_out, ct_mm, chi_out, clo_out = sems("cn_out ct_mm chi_out clo_out")
        idx_mm, relu_out, score_out, top_step, drop_out = sems("idx_mm relu_out score_out top_step drop_out")
        va_mm, va_out, vf_mm, vf_out = sems("va_mm va_out vf_mm vf_out")
        qk_mm, lg_out, mt_out, nm_out, pr_out = sems("qk_mm lg_out mt_out nm_out pr_out")
        tr_mm, prT_out, pv_mm = sems("tr_mm prT_out pv_mm")
        rinv_out, o_out, ot_mm, othi_out, otlo_out = sems("rinv_out o_out ot_mm othi_out otlo_out")
        (fin_out,) = sems("fin_out")

        def chunk(l, k, i=0):
            return l * LC + i * 2 + k

        def arrivals(l, k, i=0):
            return (l * (LC // 2) + i + (k // 2 + 1)) * 16

        block = ctx.enter_context(nc.Block())

        @block.sync
        def _(sp):
            sp.dma_start(xn[:, :, :], x).then_inc(x_in, 16)
            sp.dma_start(cst[:, 0:C_RB], consts).then_inc(const_in, 16)
            sp.dma_start(rb, rel_bias).then_inc(rb_in, 16)
            sp.dma_start(gains_all[:, :, :], gains).then_inc(gain_in, 16)

            def load(s, i):
                sp.dma_start(raw[:, s, :], stream[bass.ds(i * 2 + s, 1)].rearrange("a p n -> (a p) n")
                             ).then_inc(raw_in[s], 16)

            def reload(i):
                for s in range(2):
                    sp.wait_ge(w_back, i * 2 + s - 1)
                    load(s, i)

            for s in range(2):
                load(s, 0)
            sp.wait_ge(tab_sb, NH)
            sp.dma_start(table.rearrange("h (p y) -> p h y", y=TAB), tab).then_inc(table_out, 16)
            reload(1)
            sp.wait_ge(table_out, 16)
            skew = table[:, P - 1:P - 1 + P * (TAB - 1)].rearrange("h (p y) -> p h y", y=TAB - 1)
            sp.dma_start(bias[:, :, :], skew[:, :, 0:S]).then_inc(bias_in, 16)
            sp.dma_start(fgain[:, :], final_gain).then_inc(fgain_in, 16)
            with sp.Fori(2, NCHUNK // 2) as i:
                reload(i)
            for b in range(NB):
                sp.wait_ge(fin_out, b + 1)
                sp.dma_start(out[b], xn[:, b, :]).then_inc(out_done, 16)
            sp.wait_ge(out_done, 16 * NB)

        @block.gpsimd
        def _(pool):
            nc.gpsimd.memset(mhalf[:], -0.5).then_inc(half_set, 1)
            pool.wait_ge(half_set, 1)

            def power(n):
                for b in range(NB):
                    pool.wait_ge(ms_out, n * NB + b + 1)
                    nc.gpsimd.tensor_tensor(rstd[:, b:b + 1], ms[:, b:b + 1], mhalf[:, b:b + 1],
                                            ALU.pow).then_inc(rstd_out, 1)

            with pool.Fori(0, DEPTH) as l:
                power(l * 3)
                power(l * 3 + 1)
                pool.wait_ge(cms_out, l + 1)
                nc.gpsimd.tensor_tensor(crstd[:, :], cms[:, :], mhalf[:, :], ALU.pow).then_inc(crstd_out, 1)
                power(l * 3 + 2)
            power(DEPTH * 3)

        @block.scalar
        def _(act):
            def split_front(l, k, i=0, used=FRONT):
                act.wait_ge(raw_in[k % 2], arrivals(l, k, i))
                nc.scalar.copy(whi[:, k % 2, 0:used], raw[:, k % 2, 0:used]).then_inc(hi_front, 1)

            def split_back(k, used=UNIT):
                nc.scalar.copy(whi[:, k % 2, FRONT:FRONT + used],
                               raw[:, k % 2, FRONT:FRONT + used]).then_inc(hi_back, 1)

            def squares(n, b):
                act.wait_ge(x_ready, n * NB + b + 1)
                nc.scalar.activation(junk[:, b, :], X[:, b, :], ACT.Square,
                                     accum_out=ss[:, b:b + 1]).then_inc(ss_out, 1)

            def norm(n, g):
                for k in range(KT):
                    if k % 2 == 0:
                        act.wait_ge(xt_mm, n * (KT // 2) + (k // 2 + 1))
                    nc.scalar.mul(xhi[:, k, :], ps[:, 4 + k // 2, S * (k % 2):S * (k % 2) + S],
                                  gain[:, g + k:g + k + 1]).then_inc(xhi_out, 1)

            def ffn(l, phase):
                k0 = phase * (NF + MIXC)

                def step(f, i=0, ahead=FRONT, back=UNIT):
                    s, n = f % 2, l * (2 * NF) + i * 2 + (phase * NF + f)
                    if ahead:
                        if f > 0:
                            act.wait_ge(front_done, n)
                        split_front(l, k0 + f + 1, i, ahead)
                    act.wait_ge(front_done, n + 1)
                    nc.scalar.activation(sig[:, s, :], ps[:, GU + s, 0:S], ACT.Sigmoid).then_inc(sig_out, 1)
                    if ahead:
                        if f > 0:
                            act.wait_ge(back_done, n)
                        split_back(k0 + f + 1, back)
                    act.wait_ge(h_out, n + 1)
                    nc.scalar.copy(hhi[:, s, :], hf[:, s, :]).then_inc(hhi_out, 1)

                step(0)
                step(1)
                with act.Fori(0, NF // 2 - 2) as i:
                    step(2, i)
                    step(3, i)
                step(NF - 2)
                step(NF - 1, 0, *(MIX_USED[0] if phase == 0 else (0, 0)))

            def mix(l):
                def front(m):
                    split_front(l, NF + m, used=MIX_USED[m][0] if m < MIXC else FRONT)

                def back(m):
                    split_back(NF + m, MIX_USED[m][1] if m < MIXC else UNIT)

                def tile_out(j):
                    act.wait_ge(feat_mm, l * NFEAT + j + 1)
                    nc.scalar.copy(feat[:, j, :], ps[:, GU + j % 2, 0:S]).then_inc(feat_out, 1)

                def probs(hh):
                    act.wait_ge(nm_out, l * 2 * NH + hh + 1)
                    s = hh % 2
                    nc.scalar.activation(pr[:, s, 0:P], lg[:, s, 0:P], ACT.Exp, bias=nm[:, s, 0:1],
                                         scale=SCALE, accum_out=rsum[:, 0, hh:hh + 1])
                    nc.scalar.activation(pr[:, s, P:S3], lg[:, s, P:S3], ACT.Exp, bias=nm[:, s, 1:2],
                                         scale=SCALE, accum_out=rsum[:, 1, hh:hh + 1]).then_inc(pr_out, 1)

                def out_high(t):
                    act.wait_ge(ot_mm, l * 4 + t + 1)
                    nc.scalar.copy(xhi[:, 2 * t:2 * t + 2, :].rearrange("p a t -> p (a t)"),
                                   ps[:, 2 + t, :]).then_inc(othi_out, 1)

                act.wait_ge(table_out, 16)
                front(1)
                tile_out(KI)
                for b in range(NB):
                    act.wait_ge(c_mm, l + 1)
                    nc.scalar.activation(junk[:, b, 0:P], ps[:, CB, b * P:(b + 1) * P], ACT.Square,
                                         accum_out=css[:, b:b + 1]).then_inc(css_out, 1)
                back(1)
                act.wait_ge(az_out, l + 1)
                nc.scalar.activation(ez[:], az[:], ACT.Exp, scale=-1.0).then_inc(ez_out, 1)
                act.wait_ge(ez_out, l + 1)
                nc.scalar.activation(lz[:], ez[:], ACT.Ln, bias=1.0).then_inc(lz_out, 1)
                act.wait_ge(wf_mm, l + 1)
                front(2)
                tile_out(QI)
                act.wait_ge(crstd_out, l + 1)
                for b in range(NB):
                    nc.scalar.mul(cn[:, b, :], ps[:, CB, b * P:(b + 1) * P], crstd[:, b:b + 1]).then_inc(cn_out, 1)
                tile_out(QI + 1)
                back(2)
                tile_out(QI + 2)
                front(3)
                tile_out(QI + 3)
                act.wait_ge(ct_mm, l + 1)
                nc.scalar.mul(chi[:, :], ps[:, 6, 0:S], gain[:, G_CKV:G_CKV + 1]).then_inc(chi_out, 1)
                for h in range(NH):
                    act.wait_ge(idx_mm, l * NH + h + 1)
                    if h >= 2:
                        act.wait_ge(score_out, l * NH + h - 1)
                    nc.scalar.activation(relu[:, h % 2, :], ps[:, 6 + h % 2, 0:S3], ACT.Relu,
                                         scale=SCALE).then_inc(relu_out, 1)
                back(3)
                for j in range(KA, QA):
                    tile_out(j)
                act.wait_ge(va_mm, l + 1)
                for b in range(NB):
                    nc.scalar.copy(val[:, b, 0:D // 2], ps[:, b, :]).then_inc(va_out, 1)
                tile_out(QA)
                front(4)
                tile_out(QA + 1)
                tile_out(QA + 2)
                back(4)
                tile_out(QA + 3)
                front(5)
                tile_out(FX)
                tile_out(FX + 1)
                back(5)
                for k in range(NH + 2):
                    if k == 9:
                        act.wait_ge(vf_mm, l * 4 + 3)
                    if k in (1, 4, 6, 9):
                        front({1: 6, 4: 7, 6: 8, 9: 9}[k])
                    if k in (2, 5, 7, 9):
                        back({2: 6, 5: 7, 7: 8, 9: 9}[k])
                    if k < NH:
                        probs(k)
                    if k < 6:
                        tile_out(FX + 2 + k)
                for k in range(NH + 2):
                    if k == 0:
                        act.wait_ge(vf_mm, l * 4 + 4)
                        for b in range(NB):
                            nc.scalar.copy(val[:, b, D // 2:D], ps[:, 2 + b, :]).then_inc(vf_out, 1)
                    if k < NH:
                        probs(NH + k)
                    if k == 1:
                        front(10)
                        back(10)
                        out_high(0)
                        out_high(1)
                    if k == 6:
                        act.wait_ge(wo_mm, l * 2 * KT + 4)
                        front(11)
                    if k == 8:
                        act.wait_ge(wo_mm, l * 2 * KT + 6)
                        back(11)
                out_high(2)
                out_high(3)
                act.wait_ge(wo_mm, l * 2 * KT + 10)
                front(12)
                act.wait_ge(wo_mm, l * 2 * KT + 12)
                back(12)

            for h in range(NH):
                act.wait_ge(tab_mm, h + 1)
                nc.scalar.mul(tab[:, h, :], ps[:, 6 + h % 2, 0:TAB], 1.0 / SCALE).then_inc(tab_sb, 1)
            act.wait_ge(gain_in, 16)
            with act.Fori(0, DEPTH) as l:
                squares(l * 3, 0)
                squares(l * 3, 1)
                nc.scalar.copy(gain[:, :], gains_all[:, bass.ds(l, 1), :].rearrange("p a n -> p (a n)")
                               ).then_inc(gain_set, 1)
                split_front(l, 0)
                split_back(0)
                act.wait_ge(gain_set, l + 1)
                norm(l * 3, G_FFN1)
                ffn(l, 0)
                squares(l * 3 + 1, 0)
                squares(l * 3 + 1, 1)
                norm(l * 3 + 1, G_MIX)
                mix(l)
                squares(l * 3 + 2, 0)
                squares(l * 3 + 2, 1)
                norm(l * 3 + 2, G_FFN2)
                ffn(l, 1)
            for b in range(NB):
                squares(DEPTH * 3, b)

        @block.tensor
        def _(pe):
            def three(out_, a, b, start, stop):
                nc.tensor.matmul(out_, a[0], b[0], start=start, stop=False)
                nc.tensor.matmul(out_, a[0], b[1], start=False, stop=False)
                return nc.tensor.matmul(out_, a[1], b[0], start=False, stop=stop)

            def w(s, at, n):
                return whi[:, s, at:at + n], wlo[:, s, at:at + n]

            def xt(k, b=None):
                at = slice(0, S) if b is None else slice(b * P, (b + 1) * P)
                return xhi[:, k, at], xlo[:, k, at]

            def front_here(l, k, i=0):
                pe.wait_ge(w_front, chunk(l, k, i) + 1)

            def back_here(l, k, i=0):
                pe.wait_ge(w_back, chunk(l, k, i) + 1)

            def norm(n):
                for b in range(NB):
                    pe.wait_ge(xn_out, n * NB + b + 1)
                    for k in range(KT):
                        t = nc.tensor.transpose(ps[:, 4 + k // 2, S * (k % 2) + b * P:S * (k % 2) + (b + 1) * P],
                                                xn[:, b, k * P:(k + 1) * P], ident)
                        if b == NB - 1 and k % 2 == 1:
                            t.then_inc(xt_mm, 1)

            def ffn(l, phase):
                k0 = phase * (NF + MIXC)

                def up(f, i=0):
                    s, n = f % 2, l * (2 * NF) + i * 2 + (phase * NF + f)
                    front_here(l, k0 + f, i)
                    if f >= 2:
                        pe.wait_ge(h_out, n - 1)
                    for g in range(2):
                        for k in range(KT):
                            if f == 0 and g == 0 and k % 2 == 0:
                                pe.wait_ge(xlo_out, l * (3 * KT) + (2 * phase * KT + k + 2))
                            t = three(ps[:, GU + s, g * S:(g + 1) * S], w(s, g * UNIT + k * P, P), xt(k),
                                      k == 0, k == KT - 1)
                    t.then_inc(front_done, 1)

                def down(f, i=0):
                    s, n = f % 2, l * (2 * NF) + i * 2 + (phase * NF + f)
                    back_here(l, k0 + f, i)
                    pe.wait_ge(hlo_out, n + 1)
                    for b in range(NB):
                        h = (hhi[:, s, b * P:(b + 1) * P], hlo[:, s, b * P:(b + 1) * P])
                        for j in range(2):
                            t = three(ps[:, 2 * b + j, :], h, w(s, FRONT + j * 512, 512), f == 0, f == NF - 1)
                        if f == NF - 1 and b == 0:
                            t.then_inc(acc_mm, 1)
                    t.then_inc(back_done, 1)

                up(0)
                up(1)
                down(0)
                with pe.Fori(0, NF // 2 - 2) as i:
                    up(2, i)
                    down(1, i)
                    up(3, i)
                    down(2, i)
                up(NF - 2)
                down(NF - 3)
                up(NF - 1)
                down(NF - 2)
                down(NF - 1)

            def mix(l):
                def front(m):
                    front_here(l, NF + m)
                    return m % 2

                def back(m):
                    back_here(l, NF + m)
                    return m % 2

                def tile(j, s, at):
                    if j >= 2:
                        pe.wait_ge(feat_out, l * NFEAT + (j - 1))
                    for k in range(KT):
                        if j == KI and k % 2 == 0:
                            pe.wait_ge(xlo_out, l * (3 * KT) + (KT + k + 2))
                        t = three(ps[:, GU + j % 2, 0:S], w(s, at + k * P, P), xt(k), k == 0, k == KT - 1)
                    t.then_inc(feat_mm, 1)

                def value(u, s, at):
                    for b in range(NB):
                        for kk in range(2):
                            t = three(ps[:, 2 + b, :], xt(2 * u + kk, b), w(s, at + kk * 512, 512),
                                      2 * u + kk == 0, 2 * u + kk == KT - 1)
                    t.then_inc(vf_mm, 1)

                def project(k, b, s, at):
                    for j in range(2):
                        t = three(ps[:, 2 * b + j, :], xt(k, b), w(s, at + j * 512, 512), k == 0, k == KT - 1)
                    t.then_inc(wo_mm, 1)

                def logits(hh, bank):
                    g, h = divmod(hh, NH)
                    q, key = (QA + h // 2, KA + h // 2) if g == 0 else (FX + h // 2 * 2, FX + h // 2 * 2 + 1)
                    rows = slice(HD * (h % 2), HD * (h % 2) + HD)
                    if g == 0:
                        nc.tensor.matmul(ps[:, bank, 0:S3], nident[:], drop[:], start=True, stop=True)
                    else:
                        nc.tensor.matmul(ps[:, bank, 0:S3], pick[:, h, :], ncum[:, :], start=True, stop=True)
                    nc.tensor.matmul(ps[:, bank, 0:P], feat[rows, q, 0:P], feat[rows, key, 0:P],
                                     start=False, stop=True, skip_group_check=True)
                    nc.tensor.matmul(ps[:, bank, P:S3], feat[rows, q, P:S], feat[rows, key, :],
                                     start=False, stop=True, skip_group_check=True).then_inc(qk_mm, 1)

                def turn(hh, bank):
                    pe.wait_ge(pr_out, l * 2 * NH + (hh + 1))
                    for j in range(3):
                        t = nc.tensor.transpose(ps[:, bank, j * P:(j + 1) * P], pr[:, hh % 2, j * P:(j + 1) * P], ident)
                    t.then_inc(tr_mm, 1)

                def attend(hh, bank):
                    pe.wait_ge(prT_out, l * 2 * NH + (hh + 1))
                    o, v = slice(hh % NH * HD, (hh % NH + 1) * HD), slice(hh * HD, (hh + 1) * HD)
                    nc.tensor.matmul(ps[:, bank, o], prT[:, hh % 2, 0:P], val[:, 0, v], start=True, stop=True)
                    nc.tensor.matmul(ps[:, bank + 1, o], prT[:, hh % 2, P:2 * P], val[:, 0, v], start=True, stop=False)
                    nc.tensor.matmul(ps[:, bank + 1, o], prT[:, hh % 2, 2 * P:S3], val[:, 1, v],
                                     start=False, stop=True).then_inc(pv_mm, 1)

                def turn_outputs(g, bank):
                    pe.wait_ge(o_out, l * 2 * NB + (g + 1) * NB)
                    for t2 in range(2):
                        for k in range(2):
                            for b in range(NB):
                                at = (4 * g + 2 * t2 + k) * P
                                t = nc.tensor.transpose(ps[:, bank + t2, k * S + b * P:k * S + (b + 1) * P],
                                                        xn[:, b, at:at + P], ident)
                        t.then_inc(ot_mm, 1)

                s = front(0)
                tile(KI, s, 0)
                for b in range(NB):
                    for k in range(KT):
                        t = three(ps[:, WFB, b * 2 * NH:(b + 1) * 2 * NH], xt(k, b), w(s, UNIT + k * 2 * NH, 2 * NH),
                                  k == 0, k == KT - 1)
                t.then_inc(wf_mm, 1)
                s = back(0)
                for b in range(NB):
                    for k in range(KT):
                        t = three(ps[:, CB, b * P:(b + 1) * P], xt(k, b), w(s, FRONT + k * P, P), k == 0, k == KT - 1)
                t.then_inc(c_mm, 1)
                s = front(1)
                tile(QI, s, 0)
                tile(QI + 1, s, UNIT)
                s = back(1)
                tile(QI + 2, s, FRONT)
                s = front(2)
                tile(QI + 3, s, 0)
                pe.wait_ge(logf_out, l + 1)
                for b in range(NB):
                    nc.tensor.matmul(ps[0:NH, WFB, CUMT:CUMT + S], logf[:, b, :], tri[:, b, :], start=b == 0, stop=b == 1)
                for b in range(NB):
                    for r in range(b + 1):
                        t = nc.tensor.matmul(ps[:, WFB, CUMQ + b * NH:CUMQ + (b + 1) * NH], tri[:, r, b * P:(b + 1) * P],
                                             logf[:, r, :], start=r == 0, stop=r == b)
                t.then_inc(cum_mm, 1)
                pe.wait_ge(cn_out, l * NB + 2)
                for b in range(NB):
                    t = nc.tensor.transpose(ps[:, 6, b * P:(b + 1) * P], cn[:, b, :], ident)
                t.then_inc(ct_mm, 1)
                pe.wait_ge(feat_out, l * NFEAT + (QI + 4))
                pe.wait_ge(clo_out, l + 1)
                for h in range(NH):
                    if h >= 2:
                        pe.wait_ge(relu_out, l * NH + (h - 1))
                    rows = slice(HD * (h % 2), HD * (h % 2) + HD)
                    nc.tensor.matmul(ps[:, 6 + h % 2, 0:P], feat[rows, QI + h // 2, 0:P], feat[rows, KI, 0:P],
                                     start=True, stop=True)
                    nc.tensor.matmul(ps[:, 6 + h % 2, P:S3], feat[rows, QI + h // 2, P:S], feat[rows, KI, :],
                                     start=True, stop=True).then_inc(idx_mm, 1)
                for j in range(NH // 2):
                    pe.wait_ge(feat_out, l * NFEAT + (KA + j - 1))
                    three(ps[:, GU + (KA + j) % 2, 0:S], w(s, UNIT + j * P, P), (chi[:, :], clo[:, :]),
                          True, True).then_inc(feat_mm, 1)
                for b in range(NB):
                    t = three(ps[:, b, :], (chi[:, b * P:(b + 1) * P], clo[:, b * P:(b + 1) * P]),
                              w(s, UNIT + 512, 512), True, True)
                t.then_inc(va_mm, 1)
                s = back(2)
                tile(QA, s, FRONT)
                s = front(3)
                tile(QA + 1, s, 0)
                tile(QA + 2, s, UNIT)
                s = back(3)
                tile(QA + 3, s, FRONT)
                s = front(4)
                tile(FX, s, 0)
                tile(FX + 1, s, UNIT)
                back(4)
                pe.wait_ge(drop_out, l + 1)
                pe.wait_ge(relu_out, l * NH + NH)
                pe.wait_ge(va_out, l * NB + NB)
                pe.wait_ge(feat_out, l * NFEAT + (QA + 4))
                for k in range(NH + 2):
                    if k < NH:
                        if k >= 1:
                            pe.wait_ge(lg_out, l * 2 * NH + k)
                        logits(k, 6)
                    if k == 0:
                        tile(FX + 2, 0, FRONT)
                    elif k == 1:
                        tile(FX + 3, front(5), 0)
                    elif k == 2:
                        tile(FX + 4, 1, UNIT)
                    elif k == 3:
                        tile(FX + 5, back(5), FRONT)
                    elif k == 4:
                        tile(FX + 6, front(6), 0)
                    elif k == 5:
                        tile(FX + 7, 0, UNIT)
                    elif k == 6:
                        pe.wait_ge(cum_out, l + 1)
                        value(0, front(7), 0)
                    elif k == 7:
                        value(1, 1, UNIT)
                    elif k == 8:
                        value(2, back(7), FRONT)
                    elif k == 9:
                        value(3, front(8), 0)
                    if 1 <= k <= NH:
                        if k >= 2:
                            pe.wait_ge(prT_out, l * 2 * NH + (k - 1))
                        turn(k - 1, 7)
                    if k >= 2:
                        attend(k - 2, 0)
                pe.wait_ge(feat_out, l * NFEAT + NFEAT)
                for k in range(NH + 2):
                    if k < NH:
                        pe.wait_ge(lg_out, l * 2 * NH + (NH + k))
                        logits(NH + k, 4)
                    if k == 2:
                        front(9)
                        pe.wait_ge(otlo_out, l * 4 + 2)
                        pe.wait_ge(vf_out, l * NB + NB)
                    if k == 6:
                        back(9)
                    if k == 8:
                        front(10)
                    if k >= 2:
                        u, b = divmod(k - 2, NB)
                        project(u, b, (9 + u // 3) % 2, u % 3 * UNIT)
                    if 1 <= k <= NH:
                        pe.wait_ge(prT_out, l * 2 * NH + (NH + k - 1))
                        turn(NH + k - 1, 5)
                    if k == 1:
                        turn_outputs(0, 2)
                    if k >= 2:
                        attend(NH + k - 2, 6)
                turn_outputs(1, 4)
                for u in range(4, KT):
                    if u == 4:
                        pe.wait_ge(otlo_out, l * 4 + 3)
                    if u == 5:
                        back(10)
                    if u == 6:
                        pe.wait_ge(otlo_out, l * 4 + 4)
                        front(11)
                    for b in range(NB):
                        project(u, b, (9 + u // 3) % 2, u % 3 * UNIT)

            pe.wait_ge(rbb_set, 1)
            for h in range(NH):
                if h >= 2:
                    pe.wait_ge(tab_sb, h - 1)
                nc.tensor.matmul(ps[:, 6 + h % 2, 0:TAB], rbb[:, h, :], onehot, start=True, stop=True).then_inc(tab_mm, 1)
            pe.wait_ge(tab_sb, NH)
            with pe.Fori(0, DEPTH) as l:
                norm(l * 3)
                ffn(l, 0)
                norm(l * 3 + 1)
                mix(l)
                norm(l * 3 + 2)
                ffn(l, 1)

        @block.vector
        def _(dve):
            def split_front(l, k, i=0, used=FRONT):
                s = k % 2
                dve.wait_ge(hi_front, chunk(l, k, i) + 1)
                nc.vector.tensor_tensor(wlo[:, s, 0:used], raw[:, s, 0:used], whi[:, s, 0:used].bitcast(F32),
                                        ALU.subtract).then_inc(w_front, 1)

            def split_back(l, k, i=0, used=UNIT):
                s, at = k % 2, slice(FRONT, FRONT + used)
                dve.wait_ge(hi_back, chunk(l, k, i) + 1)
                nc.vector.tensor_tensor(wlo[:, s, at], raw[:, s, at], whi[:, s, at].bitcast(F32),
                                        ALU.subtract).then_inc(w_back, 1)

            def wait_apart(sem_, value):
                dve.wait_ge(sem_, value)
                nc.vector.memset(spare[:], 0.0)

            def scale(n):
                for b in range(NB):
                    dve.wait_ge(ss_out, n * NB + b + 1)
                    nc.vector.tensor_scalar(ms[:, b:b + 1], ss[:, b:b + 1], 1.0 / D, EPS, ALU.mult, ALU.add
                                            ).then_inc(ms_out, 1)
                for b in range(NB):
                    dve.wait_ge(rstd_out, n * NB + b + 1)
                    nc.vector.tensor_scalar(xn[:, b, :], X[:, b, :], rstd[:, b:b + 1], None, ALU.mult).then_inc(xn_out, 1)

            def norm(n, g):
                for k in range(KT):
                    if k % 2 == 0:
                        dve.wait_ge(xhi_out, n * KT + (k + 2))
                    nc.vector.scalar_tensor_tensor(
                        out=xlo[:, k, :], in0=ps[:, 4 + k // 2, S * (k % 2):S * (k % 2) + S],
                        scalar=gain[:, g + k:g + k + 1], in1=xhi[:, k, :].bitcast(F32),
                        op0=ALU.mult, op1=ALU.subtract).then_inc(xlo_out, 1)

            def residual(b, factor):
                nc.vector.scalar_tensor_tensor(
                    out=X[:, b, :], in0=ps[:, 2 * b:2 * b + 2, :].rearrange("p a n -> p (a n)"), scalar=factor,
                    in1=X[:, b, :], op0=ALU.mult, op1=ALU.add).then_inc(x_ready, 1)

            def ffn(l, phase):
                k0 = phase * (NF + MIXC)

                def step(f, i=0, ahead=FRONT, back=UNIT):
                    s, n = f % 2, l * (2 * NF) + i * 2 + (phase * NF + f)
                    if ahead:
                        split_front(l, k0 + f + 1, i, ahead)
                    dve.wait_ge(sig_out, n + 1)
                    nc.vector.tensor_tensor(hg[:, s, :], ps[:, GU + s, 0:S], sig[:, s, :], ALU.mult).then_inc(hg_out, 1)
                    dve.wait_ge(hg_out, n + 1)
                    nc.vector.tensor_tensor(hf[:, s, :], ps[:, GU + s, S:2 * S], hg[:, s, :], ALU.mult).then_inc(h_out, 1)
                    if ahead:
                        split_back(l, k0 + f + 1, i, back)
                    dve.wait_ge(hhi_out, n + 1)
                    nc.vector.tensor_tensor(hlo[:, s, :], hf[:, s, :], hhi[:, s, :].bitcast(F32), ALU.subtract
                                            ).then_inc(hlo_out, 1)

                step(0)
                step(1)
                with dve.Fori(0, NF // 2 - 2) as i:
                    step(2, i)
                    step(3, i)
                step(NF - 2)
                step(NF - 1, 0, *(MIX_USED[0] if phase == 0 else (0, 0)))
                dve.wait_ge(acc_mm, l * 2 + (phase + 1))
                residual(0, 0.5)
                dve.wait_ge(back_done, l * (2 * NF) + (phase + 1) * NF)
                residual(1, 0.5)

            def mix(l):
                def front(m):
                    split_front(l, NF + m, used=MIX_USED[m][0] if m < MIXC else FRONT)

                def back(m):
                    split_back(l, NF + m, used=MIX_USED[m][1] if m < MIXC else UNIT)

                def take(b):
                    at = slice(0, P) if b == 0 else slice(P, S3)
                    for r in range(TOPK // 8):
                        n = l * (2 * NB * (TOPK // 8)) + 2 * (b * (TOPK // 8) + r)
                        if b or r:
                            wait_apart(top_step, n)
                        else:
                            wait_apart(score_out, l * NH + NH)
                        nc.vector.max(top8[:], score[:, at]).then_inc(top_step, 1)
                        wait_apart(top_step, n + 1)
                        nc.vector.match_replace(score[:, at], top8[:], score[:, at], TAKEN).then_inc(top_step, 1)

                def maxima(hh, bank):
                    g, h = divmod(hh, NH)
                    s = hh % 2
                    wait_apart(qk_mm, l * 2 * NH + (hh + 1))
                    for b, at, n in ((0, slice(0, P), P), (1, slice(P, S3), S)):
                        add = (bias[:, h, S - n:S] if g == 0 else cmask[:, S - n:S])
                        t = nc.vector.tensor_tensor_reduce(lg[:, s, at], ps[:, bank, at], add, 1.0, LOWEST,
                                                           ALU.add, ALU.max, mx[:, s, b:b + 1])
                    t.then_inc(lg_out, 1)
                    dve.wait_ge(lg_out, l * 2 * NH + (hh + 1))
                    if g == 0:
                        nc.vector.tensor_scalar(nm[:, s, :], mx[:, s, :], -SCALE, None, ALU.mult).then_inc(nm_out, 1)
                    else:
                        nc.vector.scalar_tensor_tensor(out=mt[:, s, :], in0=mx[:, s, :], scalar=SCALE,
                                                       in1=cumq[:, :, h], op0=ALU.mult, op1=ALU.add).then_inc(mt_out, 1)
                        dve.wait_ge(mt_out, l * NH + (h + 1))
                        nc.vector.tensor_tensor(nm[:, s, :], cumq[:, :, h], mt[:, s, :], ALU.subtract).then_inc(nm_out, 1)

                def turned(hh, bank):
                    dve.wait_ge(tr_mm, l * 2 * NH + (hh + 1))
                    nc.vector.tensor_copy(prT[:, hh % 2, :], ps[:, bank, 0:S3]).then_inc(prT_out, 1)

                def outputs(g, bank):
                    heads = slice(g * NH, (g + 1) * NH)
                    dve.wait_ge(pr_out, l * 2 * NH + (g + 1) * NH)
                    nc.vector.reciprocal(rinv[:, :, heads], rsum[:, :, heads]).then_inc(rinv_out, 1)
                    dve.wait_ge(rinv_out, l * 2 + (g + 1))
                    dve.wait_ge(pv_mm, l * 2 * NH + (g + 1) * NH)
                    for b in range(NB):
                        nc.vector.tensor_tensor(
                            xn[:, b, g * 512:(g + 1) * 512].rearrange("p (h d) -> p h d", h=NH),
                            ps[:, bank + b, :].rearrange("p (h d) -> p h d", h=NH),
                            rinv[:, b, heads].unsqueeze(2).to_broadcast([P, NH, HD]), ALU.mult).then_inc(o_out, 1)

                def out_low(t, bank):
                    dve.wait_ge(othi_out, l * 4 + (t + 1))
                    at = slice(2 * t, 2 * t + 2)
                    nc.vector.tensor_tensor(xlo[:, at, :].rearrange("p a t -> p (a t)"), ps[:, bank, :],
                                            xhi[:, at, :].rearrange("p a t -> p (a t)").bitcast(F32),
                                            ALU.subtract).then_inc(otlo_out, 1)

                front(1)
                dve.wait_ge(wf_mm, l + 1)
                both = ps[:, WFB, 0:NB * 2 * NH].rearrange("p (b n) -> p b n", b=NB)
                nc.vector.tensor_scalar(wf[:], both[:, :, 0:NH], W_SCALE, None, ALU.mult)
                nc.vector.tensor_tensor(zf[:], both[:, :, NH:2 * NH],
                                        gain[:, G_BF:G_BF + NH].unsqueeze(1).to_broadcast([P, NB, NH]),
                                        ALU.add).then_inc(z_out, 1)
                dve.wait_ge(z_out, l + 1)
                nc.vector.tensor_scalar(mz[:], zf[:], 0.0, None, ALU.min)
                nc.vector.scalar_tensor_tensor(out=az[:], in0=zf[:], scalar=-1.0, in1=zf[:], op0=ALU.mult,
                                               op1=ALU.max).then_inc(az_out, 1)
                back(1)
                dve.wait_ge(css_out, l * NB + NB)
                nc.vector.tensor_scalar(cms[:], css[:], 1.0 / P, EPS, ALU.mult, ALU.add).then_inc(cms_out, 1)
                front(2)
                dve.wait_ge(lz_out, l + 1)
                nc.vector.tensor_tensor(logf[:], mz[:], lz[:], ALU.subtract).then_inc(logf_out, 1)
                back(2)
                front(3)
                dve.wait_ge(cum_mm, l + 1)
                nc.vector.tensor_scalar(ncum[:, 0:P], ps[0:NH, WFB, CUMT:CUMT + P], -1.0 / SCALE, None, ALU.mult)
                nc.vector.tensor_scalar(ncum[:, P:S3], ps[0:NH, WFB, CUMT:CUMT + S], -1.0 / SCALE, None, ALU.mult)
                nc.vector.tensor_copy(cumq[:].rearrange("p b h -> p (b h)"),
                                      ps[:, WFB, CUMQ:CUMQ + NB * NH]).then_inc(cum_out, 1)
                dve.wait_ge(chi_out, l + 1)
                nc.vector.scalar_tensor_tensor(out=clo[:], in0=ps[:, 6, 0:S], scalar=gain[:, G_CKV:G_CKV + 1],
                                               in1=chi[:].bitcast(F32), op0=ALU.mult, op1=ALU.subtract
                                               ).then_inc(clo_out, 1)
                for h in range(NH):
                    dve.wait_ge(relu_out, l * NH + (h + 1))
                    if h:
                        dve.wait_ge(score_out, l * NH + h)
                    for b, at, n in ((0, slice(0, P), P), (1, slice(P, S3), S)):
                        t = nc.vector.scalar_tensor_tensor(
                            out=score[:, at], in0=relu[:, h % 2, at], scalar=wf[:, b, h:h + 1],
                            in1=score[:, at] if h else cmask[:, S - n:S], op0=ALU.mult, op1=ALU.add)
                    t.then_inc(score_out, 1)
                back(3)
                take(0)
                front(4)
                back(4)
                take(1)
                dve.wait_ge(top_step, (l + 1) * (2 * NB * (TOPK // 8)))
                nc.vector.scalar_tensor_tensor(out=drop[:], in0=score[:], scalar=TAKEN, in1=noncausal,
                                               op0=ALU.not_equal, op1=ALU.max).then_inc(drop_out, 1)
                front(5)
                back(5)
                for k in range(NH + 2):
                    if k in (1, 4, 6, 9):
                        front({1: 6, 4: 7, 6: 8, 9: 9}[k])
                    if k in (2, 5, 7, 9):
                        back({2: 6, 5: 7, 7: 8, 9: 9}[k])
                    if k < NH:
                        maxima(k, 6)
                    if 1 <= k <= NH:
                        turned(k - 1, 7)
                for k in range(NH + 2):
                    if k < NH:
                        maxima(NH + k, 4)
                    if k == 0:
                        outputs(0, 0)
                    if 1 <= k <= NH:
                        turned(NH + k - 1, 5)
                    if k == 1:
                        front(10)
                        back(10)
                        out_low(0, 2)
                        out_low(1, 3)
                    if k == 6:
                        front(11)
                    if k == 8:
                        back(11)
                outputs(1, 6)
                out_low(2, 4)
                out_low(3, 5)
                front(12)
                back(12)
                for b in range(NB):
                    dve.wait_ge(wo_mm, l * 2 * KT + (2 * KT - 1 + b))
                    residual(b, 1.0)

            dve.wait_ge(rb_in, 16)
            dve.wait_ge(const_in, 16)
            nc.vector.tensor_copy(rbb[:], rb.unsqueeze(2).to_broadcast([NBUCKET, NH, P])).then_inc(rbb_set, 1)
            nc.vector.tensor_scalar(nident[:], ident, NEG, None, ALU.mult).then_inc(nident_set, 1)
            dve.wait_ge(x_in, 16)
            for b in range(NB):
                nc.vector.tensor_copy(X[:, b, :], xn[:, b, :]).then_inc(x_ready, 1)
            with dve.Fori(0, DEPTH) as l:
                scale(l * 3)
                split_front(l, 0)
                split_back(l, 0)
                norm(l * 3, G_FFN1)
                ffn(l, 0)
                scale(l * 3 + 1)
                norm(l * 3 + 1, G_MIX)
                mix(l)
                scale(l * 3 + 2)
                norm(l * 3 + 2, G_FFN2)
                ffn(l, 1)
            scale(DEPTH * 3)
            dve.wait_ge(fgain_in, 16)
            for b in range(NB):
                dve.wait_ge(xn_out, (DEPTH * 3) * NB + b + 1)
                nc.vector.tensor_tensor(xn[:, b, :], xn[:, b, :], fgain[:], ALU.mult).then_inc(fin_out, 1)


def bucket(dist):
    dist, exact = max(dist, 0), NBUCKET // 2
    if dist < exact:
        return dist
    ratio = MAXDIST // exact
    steps = sum(dist ** exact >= exact ** exact * ratio ** k for k in range(1, exact + 1))
    return min(exact + steps, NBUCKET - 1)


def shape_constants():
    c = np.zeros((P, C_RB), np.float32)
    row, col = np.arange(P)[:, None], np.arange(P)[None, :]
    c[:, C_ID:C_ID + P] = row == col
    c[:, C_CM + P:C_CM + S] = np.where(col > row, np.float32(NEG), np.float32(0))
    c[:, C_NC:C_NC + P] = c[:, C_NC + 2 * P:C_NC + S3] = col > row
    for b in range(NB):
        c[:, C_U + b * S:C_U + (b + 1) * S] = b * P + row <= np.arange(S)[None, :]
    for h in range(NH):
        c[h, C_E + h * P:C_E + (h + 1) * P] = 1
    for y in range(TAB):
        c[bucket(2 * P - 1 - y), C_OH + y] = 1
    return c


def by_k(w, n):
    layers, k, cols = w.shape
    return w.reshape(layers, k // P, P, cols // n, n).transpose(0, 3, 2, 1, 4).reshape(layers, cols // n, P, -1)


def lay_out(a):
    f = np.float32
    stream = np.zeros((DEPTH, LC, P, CHUNK), f)
    for name, at in (("ffn1", 0), ("ffn2", NF + MIXC)):
        stream[:, at:at + NF, :, 0:UNIT] = by_k(a[name + "_gate"], P)
        stream[:, at:at + NF, :, UNIT:FRONT] = by_k(a[name + "_up"], P)
        stream[:, at:at + NF, :, FRONT:] = a[name + "_down"].reshape(DEPTH, NF, P, D)
    w = a["w_in"]
    hw = NH * HD
    at = np.cumsum([0, hw, P, NH * HD, HD, NH, hw, hw, hw, NH])
    qa, c, qi, ki, wi, fq, fk, fv, fl = (w[:, :, at[i]:at[i + 1]] for i in range(9))
    qa, qi, fq, fk = (by_k(t, P) for t in (qa, qi, fq, fk))
    fv = by_k(fv, hw)[:, 0]
    wo = a["w_out"].reshape(DEPTH, KT, P, D)
    place = {
        0: [by_k(np.concatenate([ki, ki], 2), P)[:, 0], by_k(np.concatenate([wi, fl], 2), 2 * NH)[:, 0],
            by_k(c, P)[:, 0]],
        1: [qi[:, 0], qi[:, 1], qi[:, 2]],
        2: [qi[:, 3], np.concatenate([a["w_uk"].reshape(DEPTH, P, hw), a["w_uv"].reshape(DEPTH, P, hw)], 2), qa[:, 0]],
        3: [qa[:, 1], qa[:, 2], qa[:, 3]],
        4: [fq[:, 0], fk[:, 0], fq[:, 1]],
        5: [fk[:, 1], fq[:, 2], fk[:, 2]],
        6: [fq[:, 3], fk[:, 3]],
        7: [fv[:, :, i * UNIT:(i + 1) * UNIT] for i in range(3)],
        8: [fv[:, :, 3 * UNIT:]],
        9: [wo[:, 0], wo[:, 1], wo[:, 2]],
        10: [wo[:, 3], wo[:, 4], wo[:, 5]],
        11: [wo[:, 6], wo[:, 7]],
    }
    for m, parts in place.items():
        for i, part in enumerate(parts):
            stream[:, NF + m, :, i * UNIT:i * UNIT + part.shape[2]] = part
    gains = np.zeros((P, DEPTH, NG), f)
    for name, col in (("ffn1_norm", G_FFN1), ("mix_norm", G_MIX), ("ffn2_norm", G_FFN2)):
        gains[:, :, col:col + KT] = a[name].reshape(DEPTH, KT, P).transpose(2, 0, 1)
    gains[:, :, G_CKV] = a["ckv_norm"].T
    gains[:, :, G_BF:] = a["b_forget"][None]
    return {
        "x": np.ascontiguousarray(a["x"].reshape(NB, P, D).transpose(1, 0, 2)),
        "stream": stream.reshape(NCHUNK, P, CHUNK),
        "gains": gains,
        "final_gain": np.ascontiguousarray(np.broadcast_to(a["final_norm"][None], (P, D))),
        "consts": shape_constants(),
        "rel_bias": np.ascontiguousarray(a["rel_bias"]),
    }


def kernel(**inputs):
    import concourse.bacc as bacc
    from concourse.bass_utils import run_bass_kernel_spmd

    arrays = lay_out({k: np.asarray(v) for k, v in inputs.items()})
    nc = bacc.Bacc("TRN2", target_bir_lowering=False, num_devices=1)
    args = [nc.dram_tensor(k, v.shape, F32, kind="ExternalInput").ap() for k, v in arrays.items()]
    out = nc.dram_tensor("out", (NB, P, D), F32, kind="ExternalOutput").ap()
    table = nc.dram_tensor("table", (NH, P * TAB), F32, kind="Internal").ap()
    trunk(nc, *args, out, table)
    r = run_bass_kernel_spmd(nc, [arrays], core_ids=[0])
    return r.results[0]["out"].reshape(1, S, D)
```

```python
from contextlib import ExitStack

import numpy as np

import concourse.bass as bass
from concourse import mybir

F32 = mybir.dt.float32
F32R = mybir.dt.float32r
BF16 = mybir.dt.bfloat16
ALU = mybir.AluOpType
ACT = mybir.ActivationFunctionType

P = 128
D = 1024
S = 256
S3 = 3 * P
DEPTH = 2
NB = S // P
KT = D // P
HD = 64
NH = 8
TOPK = S // 4
DFF = ((8 * D // 3 + P - 1) // P) * P
NF = DFF // P
NBUCKET = 32
MAXDIST = 128
EPS = 1e-6
NEG = -1e30
TAKEN = -3e38
LOWEST = -3.4e38
SCALE = HD ** -0.5
W_SCALE = NH ** -0.5

UNIT = 1024
FRONT = 2 * UNIT
CHUNK = 3 * UNIT
MIXC = 12
LC = 2 * NF + MIXC
NCHUNK = DEPTH * LC
TAB = 384
TINY = 8
KW = HD + 2 * NH

MIX_USED = [(KT * (P + KW), TINY), (FRONT, UNIT), (FRONT, UNIT), (FRONT, UNIT), (FRONT, UNIT), (FRONT, UNIT),
            (FRONT, TINY), (FRONT, UNIT), (UNIT, TINY), (FRONT, UNIT), (FRONT, UNIT), (UNIT, UNIT)]

KI, QI, KA, QA, FX = 0, 1, 5, 9, 13
NFEAT = 21
NTILE = NFEAT - (QA - KA)

G_FFN1, G_MIX, G_FFN2, G_CKV, G_BF = 0, KT, 2 * KT, 3 * KT, 3 * KT + 1
NG = G_BF + NH
C_ID = 0
C_OH = C_ID + P
C_RB = C_OH + TAB
C_CM = C_RB + NH
C_NC = C_CM + S
C_U = C_NC + S3
C_E = C_U + NB * S
NC = C_E + NH * P


def trunk(nc, x, stream, gains, final_gain, consts, rel_bias, out, table):
    with ExitStack() as ctx:
        def sb(name, shape, dt=F32):
            return ctx.enter_context(nc.sbuf_tensor(name, shape, dt))

        def sems(names):
            return [ctx.enter_context(nc.semaphore(n)) for n in names.split()]

        raw = sb("raw", [P, 2, CHUNK])
        whi = sb("whi", [P, 2, CHUNK], F32R)
        wlo = sb("wlo", [P, 2, CHUNK], F32R)
        X = sb("X", [P, NB, D])
        xn = sb("xn", [P, NB, D])
        xhi = sb("xhi", [P, KT, S], F32R)
        xlo = sb("xlo", [P, KT, S], F32R)
        ones = sb("ones", [P, P])
        diag = sb("diag", [P, NB, P])
        rows = sb("rows", [P, S])
        ur = sb("ur", [P, 2, S])
        ht = sb("ht", [P, 2, S])
        pickr = sb("pickr", [NH, NH, P], F32R)
        nchi = sb("nchi", [NH, S3], F32R)
        nclo = sb("nclo", [NH, S3], F32R)
        ss = sb("ss", [P, NB])
        ms = sb("ms", [P, NB])
        rstd = sb("rstd", [P, NB])
        mhalf = sb("mhalf", [P, NB])
        gains_all = sb("gains_all", [P, DEPTH, NG])
        gain = sb("gain", [P, NG])
        fgain = sb("fgain", [P, D])
        sig = sb("sig", [P, 2, S])
        hg = sb("hg", [P, 2, S])
        hf = sb("hf", [P, 2, S])
        hhi = sb("hhi", [P, 2, S], F32R)
        hlo = sb("hlo", [P, 2, S], F32R)
        cst = sb("cst", [P, NC])
        nident = sb("nident", [P, P], BF16)
        bias = sb("bias", [P, NH, S])
        feat = sb("feat", [P, NFEAT, S])
        val = sb("val", [P, NB, D])
        wft = sb("wft", [2 * NH, S])
        wf = sb("wf", [P, NB, NH])
        zf = sb("zf", [P, NB, NH])
        az = sb("az", [P, NB, NH])
        mz = sb("mz", [P, NB, NH])
        ez = sb("ez", [P, NB, NH])
        lz = sb("lz", [P, NB, NH])
        logf = sb("logf", [P, NB, NH])
        ncum = sb("ncum", [NH, S3])
        cumq = sb("cumq", [P, NB, NH])
        cms = sb("cms", [P, NB])
        crstd = sb("crstd", [P, NB])
        chi = sb("chi", [P, S], F32R)
        clo = sb("clo", [P, S], F32R)
        relu = sb("relu", [P, 2, S3])
        score = sb("score", [P, S3])
        top8 = sb("top8", [P, NB, 8])
        drop = sb("drop", [P, S3], BF16)
        lg = sb("lg", [P, 2, S3])
        mx = sb("mx", [P, 2, NB])
        mt = sb("mt", [P, 2, NB])
        nm = sb("nm", [P, 2, NB])
        ct, csq, cn = (t[:, 0, :] for t in (hg, sig, hf))
        pr = sb("pr", [P, 2, S3])
        prT = sb("prT", [P, 2, S3])
        rsum = sb("rsum", [P, NB, 2 * NH])
        rinv = sb("rinv", [P, NB, 2 * NH])
        warm = sb("warm", [P, NB])
        spare = sb("spare", [P, 2 * NB])

        ident = cst[:, C_ID:C_ID + P]
        cmask = cst[:, C_CM:C_CM + S]
        noncausal = cst[:, C_NC:C_NC + S3]
        tri = cst[:, C_U:C_U + NB * S].rearrange("p (b t) -> p b t", b=NB)
        pick = cst[0:NH, C_E:C_E + NH * P].rearrange("p (h q) -> p h q", h=NH)
        onehot = cst[0:NBUCKET, C_OH:C_OH + TAB]
        rb = cst[0:NBUCKET, C_RB:C_RB + NH]
        rbhi, rblo = (wlo[0:NBUCKET, 1, i * NH * P:(i + 1) * NH * P].rearrange("p (h q) -> p h q", h=NH)
                      for i in range(2))
        onehot_r = wlo[0:NBUCKET, 1, FRONT:FRONT + TAB]
        tab = feat[:, 0:12, :].rearrange("p a t -> p (a t)").rearrange("p (h y) -> p h y", h=NH)

        ps = ctx.enter_context(nc.psum_tensor("ps", [P, 8, 512], F32))
        GU = 4
        ROWS = 7
        CB = 2
        WFB = 3
        SUM, CUMQ = 1, S

        front_in, back_in = sems("front_in0 front_in1"), sems("back_in0 back_in1")
        x_in = sems("x_in0 x_in1")
        table_in, const_in, rb_in, gain_in, fgain_in = sems("table_in const_in rb_in gain_in fgain_in")
        table_out, bias_in, out_done = sems("table_out bias_in out_done")
        half_set, nident_set, rb_set, gain_set, tab_mm, tab_sb = sems(
            "half_set nident_set rb_set gain_set tab_mm tab_sb")
        hi_front, hi_back = sems("hi_front hi_back")
        w_front, w_back = sems("w_front w_back")
        front_done, back_done = sems("front_done back_done")
        x_ready, ss_out, ms_out, rstd_out, diag_out, rows_mm, rows_out = sems(
            "x_ready ss_out ms_out rstd_out diag_out rows_mm rows_out")
        ones_set, pickr_set, ur_out, ht_out, nchi_out = sems("ones_set pickr_set ur_out ht_out nchi_out")
        xt_mm, xhi_out, xlo_out = sems("xt_mm xhi_out xlo_out")
        sig_out, hg_out, h_out, hhi_out, hlo_out, acc_mm = sems("sig_out hg_out h_out hhi_out hlo_out acc_mm")
        feat_mm, feat_out, ka_out, wo_mm = sems("feat_mm feat_out ka_out wo_mm")
        ncum_out, nclo_out, z_out, az_out, ez_out, lz_out, logf_out = sems("ncum_out nclo_out z_out az_out ez_out lz_out logf_out")
        cum_mm, cum_out = sems("cum_mm cum_out")
        c_mm, ct_out, csq_out, css_mm, cms_out, crstd_out, cdiag_out, crows_mm = sems(
            "c_mm ct_out csq_out css_mm cms_out crstd_out cdiag_out crows_mm")
        wft_out, wf_mm, cn_out, chi_out, clo_out = sems("wft_out wf_mm cn_out chi_out clo_out")
        idx_mm, relu_out, score_out, top_step, drop_out = sems("idx_mm relu_out score_out top_step drop_out")
        va_mm, va_out, vf_mm, vf_out = sems("va_mm va_out vf_mm vf_out")
        qk_mm, lg_out, mt_out, nm_out, pr_out = sems("qk_mm lg_out mt_out nm_out pr_out")
        tr_mm, prT_out, pv_mm = sems("tr_mm prT_out pv_mm")
        rinv_out, o_out, ot_mm, othi_out, otlo_out = sems("rinv_out o_out ot_mm othi_out otlo_out")
        (fin_out,) = sems("fin_out")

        def chunk(l, k, i=0):
            return l * LC + i * 2 + k

        def arrivals(l, k, i=0):
            return (l * (LC // 2) + i + (k // 2 + 1)) * 16

        block = ctx.enter_context(nc.Block())

        @block.sync
        def _(sp):
            sp.dma_start(cst[:, 0:C_RB], consts[:, 0:C_RB]).then_inc(table_in, 16)
            sp.dma_start(rb, rel_bias).then_inc(rb_in, 16)
            for b in range(NB):
                sp.dma_start(X[:, b, :], x[:, b, :]).then_inc(x_in[b], 16)
            sp.dma_start(gains_all[:, :, :], gains).then_inc(gain_in, 16)

            def load_front(s, i):
                sp.dma_start(raw[:, s, 0:FRONT], stream[bass.ds(i * 2 + s, 1), :, 0:FRONT].rearrange(
                    "a p n -> (a p) n")).then_inc(front_in[s], 16)

            def load_back(s, i):
                sp.dma_start(raw[:, s, FRONT:CHUNK], stream[bass.ds(i * 2 + s, 1), :, FRONT:CHUNK].rearrange(
                    "a p n -> (a p) n")).then_inc(back_in[s], 16)

            def reload(i):
                for s in range(2):
                    sp.wait_ge(w_front, (i * 2 + s - 1) * 2)
                    load_front(s, i)
                    sp.wait_ge(w_back, i * 2 + s - 1)
                    load_back(s, i)

            for s in range(2):
                load_front(s, 0)
                load_back(s, 0)
            sp.dma_start(cst[:, C_CM:NC], consts[:, C_CM:NC]).then_inc(const_in, 16)
            sp.wait_ge(tab_sb, NH)
            sp.dma_start(table.rearrange("h (p y) -> p h y", y=TAB), tab).then_inc(table_out, 16)
            reload(1)
            sp.wait_ge(table_out, 16)
            skew = table[:, P - 1:P - 1 + P * (TAB - 1)].rearrange("h (p y) -> p h y", y=TAB - 1)
            sp.dma_start(bias[:, :, :], skew[:, :, 0:S]).then_inc(bias_in, 16)
            sp.dma_start(fgain[:, :], final_gain).then_inc(fgain_in, 16)
            with sp.Fori(2, NCHUNK // 2) as i:
                reload(i)
            for b in range(NB):
                sp.wait_ge(fin_out, b + 1)
                sp.dma_start(out[b], xn[:, b, :]).then_inc(out_done, 16)
            sp.wait_ge(out_done, 16 * NB)

        @block.gpsimd
        def _(pool):
            nc.gpsimd.memset(mhalf[:], -0.5).then_inc(half_set, 1)
            pool.wait_ge(half_set, 1)

            def power(n):
                for b in range(NB):
                    pool.wait_ge(ms_out, n * NB + b + 1)
                    nc.gpsimd.tensor_tensor(rstd[:, b:b + 1], ms[:, b:b + 1], mhalf[:, b:b + 1],
                                            ALU.pow).then_inc(rstd_out, 1)

            with pool.Fori(0, DEPTH) as l:
                power(l * 3)
                power(l * 3 + 1)
                pool.wait_ge(cms_out, l + 1)
                nc.gpsimd.tensor_tensor(crstd[:, :], cms[:, :], mhalf[:, :], ALU.pow).then_inc(crstd_out, 1)
                power(l * 3 + 2)
            power(DEPTH * 3)

        @block.scalar
        def _(act):
            def split_front(l, k, i=0, used=FRONT):
                act.wait_ge(front_in[k % 2], arrivals(l, k, i))
                for at in (slice(0, used // 2), slice(used // 2, used)):
                    nc.scalar.copy(whi[:, k % 2, at], raw[:, k % 2, at]).then_inc(hi_front, 1)

            def split_back(l, k, i=0, used=UNIT):
                act.wait_ge(back_in[k % 2], arrivals(l, k, i))
                nc.scalar.copy(whi[:, k % 2, FRONT:FRONT + used],
                               raw[:, k % 2, FRONT:FRONT + used]).then_inc(hi_back, 1)

            def squares(n, b):
                act.wait_ge(x_ready, n * (2 * NB) + (2 * b + 2))
                nc.scalar.activation(xn[:, b, :], X[:, b, :], ACT.Square,
                                     accum_out=ss[:, b:b + 1]).then_inc(ss_out, 1)

            def norm(n, g, l, ahead=None):
                squares(n, 0)
                for k in range(KT):
                    if k % 2 == 0:
                        act.wait_ge(xt_mm, n * (KT // 2) + (k // 2 + 1))
                    nc.scalar.mul(xhi[:, k, :], ps[:, 4 + k // 2, S * (k % 2):S * (k % 2) + S],
                                  gain[:, g + k:g + k + 1]).then_inc(xhi_out, 1)
                if ahead is not None:
                    split_front(l, ahead)
                squares(n, 1)

            def ffn(l, phase):
                k0 = phase * (NF + MIXC)

                def step(f, i=0, back=UNIT, front=FRONT):
                    s, n = f % 2, l * (2 * NF) + i * 2 + (phase * NF + f)
                    act.wait_ge(hg_out, n + 1)
                    nc.scalar.activation(sig[:, s, :], hg[:, s, :], ACT.Sigmoid).then_inc(sig_out, 1)
                    act.wait_ge(h_out, n + 1)
                    nc.scalar.copy(hhi[:, s, :], hf[:, s, :]).then_inc(hhi_out, 1)
                    if back:
                        if f > 0:
                            act.wait_ge(back_done, n)
                        split_back(l, k0 + f + 1, i, back)
                    if front:
                        act.wait_ge(front_done, n + 1)
                        split_front(l, k0 + f + 2, i, front)

                step(0)
                step(1)
                with act.Fori(0, NF // 2 - 2) as i:
                    step(2, i)
                    step(3, i)
                step(NF - 2, front=MIX_USED[0][0] if phase == 0 else 0)
                step(NF - 1, back=MIX_USED[0][1] if phase == 0 else 0, front=MIX_USED[1][0] if phase == 0 else 0)

            def mix(l):
                def front(m):
                    split_front(l, NF + m, used=MIX_USED[m][0] if m < MIXC else FRONT)

                def back(m):
                    split_back(l, NF + m, used=MIX_USED[m][1] if m < MIXC else UNIT)

                def probs(hh):
                    act.wait_ge(nm_out, l * 2 * NH + hh + 1)
                    s = hh % 2
                    nc.scalar.activation(pr[:, s, 0:P], lg[:, s, 0:P], ACT.Exp, bias=nm[:, s, 0:1],
                                         scale=SCALE, accum_out=rsum[:, 0, hh:hh + 1])
                    nc.scalar.activation(pr[:, s, P:S3], lg[:, s, P:S3], ACT.Exp, bias=nm[:, s, 1:2],
                                         scale=SCALE, accum_out=rsum[:, 1, hh:hh + 1]).then_inc(pr_out, 1)

                def out_high(t, bank):
                    act.wait_ge(ot_mm, l * 4 + t + 1)
                    nc.scalar.copy(xhi[:, 2 * t:2 * t + 2, :].rearrange("p a t -> p (a t)"),
                                   ps[:, bank, :]).then_inc(othi_out, 1)

                back(1)
                act.wait_ge(ct_out, l + 1)
                nc.scalar.activation(csq, ct, ACT.Square).then_inc(csq_out, 1)
                act.wait_ge(az_out, l + 1)
                nc.scalar.activation(ez[:], az[:], ACT.Exp, scale=-1.0).then_inc(ez_out, 1)
                act.wait_ge(ez_out, l + 1)
                nc.scalar.activation(lz[:], ez[:], ACT.Ln, bias=1.0).then_inc(lz_out, 1)
                act.wait_ge(c_mm, l + 1)
                front(2)
                act.wait_ge(feat_mm, l * NFEAT + (KI + 1))
                back(2)
                act.wait_ge(feat_mm, l * NFEAT + (QI + 2))
                front(3)
                act.wait_ge(cn_out, l + 1)
                nc.scalar.mul(chi[:, :], cn, gain[:, G_CKV:G_CKV + 1]).then_inc(chi_out, 1)
                for h in range(NH):
                    act.wait_ge(idx_mm, l * NH + h + 1)
                    if h >= 2:
                        act.wait_ge(score_out, l * NH + h - 1)
                    nc.scalar.activation(relu[:, h % 2, :], ps[:, 6 + h % 2, 0:S3], ACT.Relu,
                                         scale=SCALE).then_inc(relu_out, 1)
                    if 2 <= h < 2 + (QA - KA):
                        j = KA + h - 2
                        act.wait_ge(feat_mm, l * NFEAT + j + 1)
                        nc.scalar.copy(feat[:, j, :], ps[:, GU + j % 2, 0:S]).then_inc(ka_out, 1)
                act.wait_ge(va_mm, l + 1)
                for b in range(NB):
                    nc.scalar.copy(val[:, b, 0:D // 2], ps[:, b, :]).then_inc(va_out, 1)
                back(3)
                front(4)
                act.wait_ge(feat_mm, l * NFEAT + (QA + 1))
                back(4)
                act.wait_ge(feat_mm, l * NFEAT + (QA + 3))
                front(5)
                act.wait_ge(feat_mm, l * NFEAT + (QA + 4))
                back(5)
                act.wait_ge(feat_mm, l * NFEAT + (FX + 2))
                front(6)
                act.wait_ge(feat_mm, l * NFEAT + (FX + 3))
                back(6)
                for k in range(NH + 2):
                    if k == 1:
                        act.wait_ge(feat_mm, l * NFEAT + (FX + 5))
                        front(7)
                    if k == 2:
                        act.wait_ge(feat_mm, l * NFEAT + (FX + 6))
                        back(7)
                    if k == 4:
                        act.wait_ge(feat_mm, l * NFEAT + NFEAT)
                        front(8)
                        back(8)
                    if k == 6:
                        act.wait_ge(vf_mm, l * 4 + 2)
                        front(9)
                    if k == 7:
                        act.wait_ge(vf_mm, l * 4 + 3)
                        back(9)
                    if k < NH:
                        probs(k)
                act.wait_ge(vf_mm, l * 4 + 4)
                for b in range(NB):
                    nc.scalar.mul(val[:, b, D // 2:D], ps[:, 2 + b, :], rstd[:, b:b + 1]).then_inc(vf_out, 1)
                for k in range(NH + 2):
                    if k < NH:
                        probs(NH + k)
                    if k == 0:
                        out_high(0, 0)
                        front(10)
                        back(10)
                    if k == 2:
                        out_high(1, 7)
                    if k == 6:
                        act.wait_ge(wo_mm, l * 2 * KT + 4)
                        front(11)
                    if k == 7:
                        out_high(2, 6)
                    if k == 8:
                        act.wait_ge(wo_mm, l * 2 * KT + 6)
                        back(11)
                act.wait_ge(wo_mm, l * 2 * KT + 10)
                front(12)
                out_high(3, 7)
                act.wait_ge(wo_mm, l * 2 * KT + 12)
                back(12)
                act.wait_ge(wo_mm, l * 2 * KT + 14)
                front(13)

            for h in range(NH):
                act.wait_ge(tab_mm, h + 1)
                nc.scalar.mul(tab[:, h, :], ps[:, h, 0:TAB], 1.0 / SCALE).then_inc(tab_sb, 1)
            act.wait_ge(half_set, 1)
            nc.scalar.activation(warm[:], mhalf[:, 0:NB], ACT.Sigmoid)
            act.wait_ge(gain_in, 16)
            with act.Fori(0, DEPTH) as l:
                split_front(l, 0)
                act.wait_ge(x_ready, l * (3 * 2 * NB) + 1)
                nc.scalar.copy(gain[:, :], gains_all[:, bass.ds(l, 1), :].rearrange("p a n -> p (a n)")
                               ).then_inc(gain_set, 1)
                act.wait_ge(gain_set, l + 1)
                norm(l * 3, G_FFN1, l, 1)
                split_back(l, 0)
                ffn(l, 0)
                norm(l * 3 + 1, G_MIX, l)
                mix(l)
                norm(l * 3 + 2, G_FFN2, l)
                ffn(l, 1)
            for b in range(NB):
                squares(DEPTH * 3, b)

        @block.tensor
        def _(pe):
            def three(out_, a, b, start, stop):
                nc.tensor.matmul(out_, a[0], b[0], start=start, stop=False)
                nc.tensor.matmul(out_, a[0], b[1], start=False, stop=False)
                return nc.tensor.matmul(out_, a[1], b[0], start=False, stop=stop)

            def w(s, at, n):
                return whi[:, s, at:at + n], wlo[:, s, at:at + n]

            def xt(k, b=None):
                at = slice(0, S) if b is None else slice(b * P, (b + 1) * P)
                return xhi[:, k, at], xlo[:, k, at]

            def front_here(l, k, i=0, half=1):
                pe.wait_ge(w_front, chunk(l, k, i) * 2 + (half + 1))

            def back_here(l, k, i=0):
                pe.wait_ge(w_back, chunk(l, k, i) + 1)

            def norm(n):
                for b in range(NB):
                    for k in range(KT):
                        if k % 4 == 0:
                            pe.wait_ge(x_ready, n * (2 * NB) + (2 * b + k // 4 + 1))
                        t = nc.tensor.transpose(ps[:, 4 + k // 2, S * (k % 2) + b * P:S * (k % 2) + (b + 1) * P],
                                                X[:, b, k * P:(k + 1) * P], ident)
                        if b == NB - 1 and k % 2 == 1:
                            t.then_inc(xt_mm, 1)

            def spread(bank):
                for b in range(NB):
                    t = nc.tensor.matmul(ps[:, bank, b * P:(b + 1) * P], ones[:, :], diag[:, b, :], start=True, stop=True)
                return t

            def ffn(l, phase):
                k0 = phase * (NF + MIXC)

                def up(f, i=0):
                    s, n = f % 2, l * (2 * NF) + i * 2 + (phase * NF + f)
                    if f >= 2:
                        pe.wait_ge(ur_out, n - 1)
                    for g in range(2):
                        front_here(l, k0 + f, i, g)
                        if f == 1 and g == 1:
                            pe.wait_ge(diag_out, l * 3 + (2 * phase + 1))
                            spread(ROWS).then_inc(rows_mm, 1)
                        for k in range(KT):
                            if f == 0 and g == 0 and k % 2 == 0:
                                pe.wait_ge(xlo_out, l * (3 * KT) + (2 * phase * KT + k + 2))
                            t = three(ps[:, GU + s, g * S:(g + 1) * S], w(s, g * UNIT + k * P, P), xt(k),
                                      k == 0, k == KT - 1)
                    t.then_inc(front_done, 1)

                def down(f, i=0):
                    s, n = f % 2, l * (2 * NF) + i * 2 + (phase * NF + f)
                    back_here(l, k0 + f, i)
                    pe.wait_ge(hlo_out, n + 1)
                    for b in range(NB):
                        h = (hhi[:, s, b * P:(b + 1) * P], hlo[:, s, b * P:(b + 1) * P])
                        for j in range(2):
                            t = three(ps[:, 2 * b + j, :], h, w(s, FRONT + j * 512, 512), f == 0, f == NF - 1)
                            if f == NF - 1 and (b, j) in ((0, 1), (1, 0)):
                                t.then_inc(acc_mm, 1)
                    t.then_inc(back_done, 1)

                up(0)
                up(1)
                down(0)
                with pe.Fori(0, NF // 2 - 2) as i:
                    up(2, i)
                    down(1, i)
                    up(3, i)
                    down(2, i)
                up(NF - 2)
                down(NF - 3)
                up(NF - 1)
                down(NF - 2)
                down(NF - 1)

            def mix(l):
                def front(m, half=1):
                    front_here(l, NF + m, 0, half)
                    return m % 2

                def back(m):
                    back_here(l, NF + m)
                    return m % 2

                def tile(j, s, at):
                    if QI + 1 <= j < QA:
                        pe.wait_ge(feat_out, l * NTILE + (j - 1))
                    elif QA <= j < QA + 2:
                        pe.wait_ge(ka_out, l * (QA - KA) + (j - QA + 3))
                    elif j >= QA + 2:
                        pe.wait_ge(feat_out, l * NTILE + (j - 1 - (QA - KA)))
                    for k in range(KT):
                        t = three(ps[:, GU + j % 2, 0:S], w(s, at + k * P, P), xt(k), k == 0, k == KT - 1)
                    t.then_inc(feat_mm, 1)

                def value(u, s, at):
                    for b in range(NB):
                        for kk in range(2):
                            t = three(ps[:, 2 + b, :], xt(2 * u + kk, b), w(s, at + kk * 512, 512),
                                      2 * u + kk == 0, 2 * u + kk == KT - 1)
                    t.then_inc(vf_mm, 1)

                def project(k, b, s, at):
                    for j in range(2):
                        t = three(ps[:, 2 * b + j, :], xt(k, b), w(s, at + j * 512, 512), k == 0, k == KT - 1)
                        if (k, b, j) == (KT - 1, 1, 0):
                            t.then_inc(acc_mm, 1)
                    t.then_inc(wo_mm, 1)

                def logits(hh, bank):
                    g, h = divmod(hh, NH)
                    q, key = (QA + h // 2, KA + h // 2) if g == 0 else (FX + h // 2 * 2, FX + h // 2 * 2 + 1)
                    rows = slice(HD * (h % 2), HD * (h % 2) + HD)
                    if g == 0:
                        nc.tensor.matmul(ps[:, bank, 0:S3], nident[:], drop[:], start=True, stop=True)
                    else:
                        nc.tensor.matmul(ps[:, bank, 0:S3], pickr[:, h, :], nchi[:, :], start=True, stop=False)
                        nc.tensor.matmul(ps[:, bank, 0:S3], pickr[:, h, :], nclo[:, :], start=False, stop=True)
                    nc.tensor.matmul(ps[:, bank, 0:P], feat[rows, q, 0:P], feat[rows, key, 0:P],
                                     start=False, stop=True, skip_group_check=True)
                    nc.tensor.matmul(ps[:, bank, P:S3], feat[rows, q, P:S], feat[rows, key, :],
                                     start=False, stop=True, skip_group_check=True).then_inc(qk_mm, 1)

                def turn(hh, bank):
                    pe.wait_ge(pr_out, l * 2 * NH + (hh + 1))
                    for j in range(3):
                        t = nc.tensor.transpose(ps[:, bank, j * P:(j + 1) * P], pr[:, hh % 2, j * P:(j + 1) * P], ident)
                    t.then_inc(tr_mm, 1)

                def attend(hh, bank):
                    pe.wait_ge(prT_out, l * 2 * NH + (hh + 1))
                    v, at, o = slice(hh * HD, (hh + 1) * HD), hh % 4 * HD, ps[:, bank + hh % NH // 4, :]
                    nc.tensor.matmul(o[:, at:at + HD], prT[:, hh % 2, 0:P], val[:, 0, v], start=True, stop=True)
                    nc.tensor.matmul(o[:, S + at:S + at + HD], prT[:, hh % 2, P:2 * P], val[:, 0, v], start=True, stop=False)
                    nc.tensor.matmul(o[:, S + at:S + at + HD], prT[:, hh % 2, 2 * P:S3], val[:, 1, v],
                                     start=False, stop=True).then_inc(pv_mm, 1)

                def turn_outputs(t2, bank):
                    pe.wait_ge(o_out, l * 4 + (t2 + 1))
                    for k in range(2):
                        for b in range(NB):
                            at = (2 * t2 + k) * P
                            t = nc.tensor.transpose(ps[:, bank, k * S + b * P:k * S + (b + 1) * P],
                                                    xn[:, b, at:at + P], ident)
                    t.then_inc(ot_mm, 1)

                s = front(0)
                for k in range(0, KT, 2):
                    pe.wait_ge(xlo_out, l * (3 * KT) + (KT + k + 2))
                    for kk in (k, k + 1):
                        t = three(ps[:, CB, 0:S], w(s, kk * P, P), xt(kk), kk == 0, kk == KT - 1)
                        u = three(ps[0:KW, GU + KI, 0:S], w(s, KT * P + kk * KW, KW), xt(kk), kk == 0, kk == KT - 1)
                t.then_inc(c_mm, 1)
                u.then_inc(feat_mm, 1)
                pe.wait_ge(diag_out, l * 3 + 2)
                spread(ROWS).then_inc(rows_mm, 1)
                tile(QI, front(1, 0), 0)
                pe.wait_ge(wft_out, l + 1)
                for b in range(NB):
                    t = nc.tensor.matmul(ps[:, WFB, b * 2 * NH:(b + 1) * 2 * NH], wft[:, b * P:(b + 1) * P],
                                         ident[0:2 * NH, 0:2 * NH], start=True, stop=True)
                t.then_inc(wf_mm, 1)
                pe.wait_ge(csq_out, l + 1)
                for b in range(NB):
                    t = nc.tensor.matmul(ps[:, CB, b:b + 1], csq[:, b * P:(b + 1) * P], ones[:, 0:1],
                                         start=True, stop=True)
                t.then_inc(css_mm, 1)
                tile(QI + 1, front(1), UNIT)
                pe.wait_ge(cdiag_out, l + 1)
                spread(CB).then_inc(crows_mm, 1)
                tile(QI + 2, back(1), FRONT)
                pe.wait_ge(logf_out, l + 1)
                for b in range(NB):
                    nc.tensor.matmul(ps[0:NH, SUM, 0:S], logf[:, b, :], tri[:, b, :], start=b == 0, stop=b == 1)
                for b in range(NB):
                    for r in range(b + 1):
                        t = nc.tensor.matmul(ps[:, SUM, CUMQ + b * NH:CUMQ + (b + 1) * NH], tri[:, r, b * P:(b + 1) * P],
                                             logf[:, r, :], start=r == 0, stop=r == b)
                t.then_inc(cum_mm, 1)
                s = front(2)
                tile(QI + 3, s, 0)
                for h in range(NH):
                    if h % 2 == 0:
                        pe.wait_ge(feat_out, l * NTILE + (QI + h // 2 + 1))
                    if h >= 2:
                        pe.wait_ge(relu_out, l * NH + (h - 1))
                    rows_ = slice(HD * (h % 2), HD * (h % 2) + HD)
                    nc.tensor.matmul(ps[:, 6 + h % 2, 0:P], feat[rows_, QI + h // 2, 0:P], feat[rows_, KI, 0:P],
                                     start=True, stop=True)
                    nc.tensor.matmul(ps[:, 6 + h % 2, P:S3], feat[rows_, QI + h // 2, P:S], feat[rows_, KI, :],
                                     start=True, stop=True).then_inc(idx_mm, 1)
                    if 2 <= h < 2 + (QA - KA):
                        j = KA + h - 2
                        if h == 2:
                            pe.wait_ge(clo_out, l + 1)
                        if j < KA + 2:
                            pe.wait_ge(feat_out, l * NTILE + (j - 1))
                        else:
                            pe.wait_ge(ka_out, l * (QA - KA) + (j - KA - 1))
                        three(ps[:, GU + j % 2, 0:S], w(s, UNIT + (j - KA) * P, P), (chi[:, :], clo[:, :]),
                              True, True).then_inc(feat_mm, 1)
                pe.wait_ge(cum_out, l + 1)
                for b in range(NB):
                    t = three(ps[:, b, :], (chi[:, b * P:(b + 1) * P], clo[:, b * P:(b + 1) * P]),
                              w(s, UNIT + 512, 512), True, True)
                t.then_inc(va_mm, 1)
                s = back(2)
                tile(QA, s, FRONT)
                tile(QA + 1, front(3, 0), 0)
                tile(QA + 2, front(3), UNIT)
                s = back(3)
                tile(QA + 3, s, FRONT)
                tile(FX, front(4, 0), 0)
                tile(FX + 1, front(4), UNIT)
                s = back(4)
                tile(FX + 2, s, FRONT)
                tile(FX + 3, front(5, 0), 0)
                pe.wait_ge(drop_out, l + 1)
                pe.wait_ge(relu_out, l * NH + NH)
                pe.wait_ge(va_out, l * NB + NB)
                pe.wait_ge(ka_out, (l + 1) * (QA - KA))
                pe.wait_ge(feat_out, l * NTILE + (QA + 4 - (QA - KA)))
                for k in range(NH + 2):
                    if k < NH:
                        if k >= 1:
                            pe.wait_ge(lg_out, l * 2 * NH + k)
                        logits(k, 6)
                    if k == 0:
                        tile(FX + 4, front(5), UNIT)
                    elif k == 1:
                        tile(FX + 5, back(5), FRONT)
                    elif k == 2:
                        tile(FX + 6, front(6, 0), 0)
                    elif k == 3:
                        tile(FX + 7, front(6), UNIT)
                    elif k == 4:
                        value(0, front(7, 0), 0)
                    elif k == 5:
                        value(1, front(7), UNIT)
                    elif k == 6:
                        value(2, back(7), FRONT)
                    elif k == 7:
                        value(3, front(8), 0)
                    if 1 <= k <= NH:
                        if k >= 2:
                            pe.wait_ge(prT_out, l * 2 * NH + (k - 1))
                        turn(k - 1, 7)
                    if k >= 2:
                        attend(k - 2, 0)
                    if k == 7:
                        turn_outputs(0, 0)
                pe.wait_ge(pickr_set, l + 1)
                pe.wait_ge(feat_out, l * NTILE + NTILE)
                for k in range(NH + 2):
                    if k < NH:
                        pe.wait_ge(lg_out, l * 2 * NH + (NH + k))
                        logits(NH + k, 4)
                    if k == 2:
                        front(9)
                        pe.wait_ge(otlo_out, l * 4 + 1)
                        pe.wait_ge(vf_out, l * NB + NB)
                    if k == 6:
                        back(9)
                        pe.wait_ge(otlo_out, l * 4 + 2)
                    if k == 8:
                        front(10)
                    if k >= 2:
                        u, b = divmod(k - 2, NB)
                        project(u, b, (9 + u // 3) % 2, u % 3 * UNIT)
                    if 1 <= k <= NH:
                        pe.wait_ge(prT_out, l * 2 * NH + (NH + k - 1))
                        turn(NH + k - 1, 5)
                    if k >= 2:
                        attend(NH + k - 2, 6)
                    if k == 1:
                        turn_outputs(1, 7)
                    if k == 7:
                        turn_outputs(2, 6)
                for u in range(4, KT):
                    if u == 4:
                        pe.wait_ge(otlo_out, l * 4 + 3)
                    if u == 5:
                        back(10)
                    if u == 6:
                        turn_outputs(3, 7)
                        pe.wait_ge(otlo_out, l * 4 + 4)
                        front(11)
                    if u == 7:
                        back(11)
                    for b in range(NB):
                        project(u, b, (9 + u // 3) % 2, u % 3 * UNIT if u < 7 else FRONT)

            pe.wait_ge(rb_set, 3)
            for h in range(NH):
                nc.tensor.matmul(ps[:, h, 0:TAB], rbhi[:, h, :], onehot_r, start=True, stop=False)
                nc.tensor.matmul(ps[:, h, 0:TAB], rblo[:, h, :], onehot_r, start=False, stop=True).then_inc(tab_mm, 1)
            pe.wait_ge(tab_sb, NH)
            pe.wait_ge(ones_set, 1)
            with pe.Fori(0, DEPTH) as l:
                norm(l * 3)
                ffn(l, 0)
                norm(l * 3 + 1)
                mix(l)
                norm(l * 3 + 2)
                ffn(l, 1)

        @block.vector
        def _(dve):
            def split_front(l, k, i=0, used=FRONT, halves=(0, 1)):
                for half in halves:
                    s, at = k % 2, slice(half * (used // 2), (half + 1) * (used // 2))
                    dve.wait_ge(hi_front, chunk(l, k, i) * 2 + (half + 1))
                    nc.vector.tensor_tensor(wlo[:, s, at], raw[:, s, at], whi[:, s, at].bitcast(F32),
                                            ALU.subtract).then_inc(w_front, 1)

            def split_back(l, k, i=0, used=UNIT):
                s, at = k % 2, slice(FRONT, FRONT + used)
                dve.wait_ge(hi_back, chunk(l, k, i) + 1)
                nc.vector.tensor_tensor(wlo[:, s, at], raw[:, s, at], whi[:, s, at].bitcast(F32),
                                        ALU.subtract).then_inc(w_back, 1)

            def wait_apart(sem_, value, column=0):
                dve.wait_ge(sem_, value)
                nc.vector.memset(spare[:, column:column + 1], 0.0)

            def mean(n, b):
                dve.wait_ge(ss_out, n * NB + b + 1)
                nc.vector.tensor_scalar(ms[:, b:b + 1], ss[:, b:b + 1], 1.0 / D, EPS, ALU.mult, ALU.add
                                        ).then_inc(ms_out, 1)

            def norm(n, g, l, k, first=False):
                for t in range(KT):
                    if t % 2 == 0:
                        dve.wait_ge(xhi_out, n * KT + (t + 2))
                    nc.vector.scalar_tensor_tensor(
                        out=xlo[:, t, :], in0=ps[:, 4 + t // 2, S * (t % 2):S * (t % 2) + S],
                        scalar=gain[:, g + t:g + t + 1], in1=xhi[:, t, :].bitcast(F32),
                        op0=ALU.mult, op1=ALU.subtract).then_inc(xlo_out, 1)
                mean(n, 0)
                if first:
                    split_front(l, 0, halves=(1,))
                split_front(l, k, halves=(0,))
                mean(n, 1)
                split_front(l, k, halves=(1,))
                for b in range(NB):
                    dve.wait_ge(rstd_out, n * NB + b + 1)
                    t = nc.vector.tensor_scalar(diag[:, b, :], ident, rstd[:, b:b + 1], None, ALU.mult)
                t.then_inc(diag_out, 1)
                if first:
                    split_back(l, 0)
                dve.wait_ge(rows_mm, n + 1)
                nc.vector.tensor_copy(rows[:, :], ps[:, ROWS, 0:S]).then_inc(rows_out, 1)
                dve.wait_ge(rows_out, n + 1)

            def residual(b, j, factor):
                at = slice(j * 512, (j + 1) * 512)
                nc.vector.scalar_tensor_tensor(out=X[:, b, at], in0=ps[:, 2 * b + j, :], scalar=factor,
                                               in1=X[:, b, at], op0=ALU.mult, op1=ALU.add).then_inc(x_ready, 1)

            def ffn(l, phase):
                k0 = phase * (NF + MIXC)

                def step(f, i=0, back=UNIT, front=FRONT):
                    s, n = f % 2, l * (2 * NF) + i * 2 + (phase * NF + f)
                    dve.wait_ge(front_done, n + 1)
                    nc.vector.tensor_tensor(hg[:, s, :], ps[:, GU + s, 0:S], rows[:, :], ALU.mult).then_inc(hg_out, 1)
                    nc.vector.tensor_tensor(ur[:, s, :], ps[:, GU + s, S:2 * S], rows[:, :], ALU.mult).then_inc(ur_out, 1)
                    dve.wait_ge(sig_out, n + 1)
                    nc.vector.tensor_tensor(ht[:, s, :], hg[:, s, :], sig[:, s, :], ALU.mult).then_inc(ht_out, 1)
                    dve.wait_ge(ht_out, n + 1)
                    dve.wait_ge(ur_out, n + 1)
                    nc.vector.tensor_tensor(hf[:, s, :], ht[:, s, :], ur[:, s, :], ALU.mult).then_inc(h_out, 1)
                    dve.wait_ge(hhi_out, n + 1)
                    nc.vector.tensor_tensor(hlo[:, s, :], hf[:, s, :], hhi[:, s, :].bitcast(F32), ALU.subtract
                                            ).then_inc(hlo_out, 1)
                    if back:
                        split_back(l, k0 + f + 1, i, back)
                    if front:
                        split_front(l, k0 + f + 2, i, front)

                step(0)
                step(1)
                with dve.Fori(0, NF // 2 - 2) as i:
                    step(2, i)
                    step(3, i)
                step(NF - 2, front=MIX_USED[0][0] if phase == 0 else 0)
                step(NF - 1, back=MIX_USED[0][1] if phase == 0 else 0, front=0)
                dve.wait_ge(acc_mm, l * 5 + (3 * phase + 1))
                residual(0, 0, 0.5)
                residual(0, 1, 0.5)
                dve.wait_ge(acc_mm, l * 5 + (3 * phase + 2))
                residual(1, 0, 0.5)
                dve.wait_ge(back_done, l * (2 * NF) + (phase + 1) * NF)
                residual(1, 1, 0.5)

            def mix(l):
                def front(m, halves=(0, 1)):
                    split_front(l, NF + m, used=MIX_USED[m][0] if m < MIXC else FRONT, halves=halves)

                def back(m):
                    split_back(l, NF + m, used=MIX_USED[m][1] if m < MIXC else UNIT)

                def take(r0, r1):
                    ats = slice(0, P), slice(P, S3)
                    for r in range(r0, r1):
                        n = l * (2 * NB * (TOPK // 8)) + 2 * NB * r
                        for b in range(NB):
                            if r:
                                wait_apart(top_step, n - NB + (b + 1), b)
                            elif b == 0:
                                wait_apart(score_out, l * NH + NH)
                            nc.vector.max(top8[:, b, :], score[:, ats[b]]).then_inc(top_step, 1)
                        for b in range(NB):
                            wait_apart(top_step, n + (b + 1), NB + b)
                            nc.vector.match_replace(score[:, ats[b]], top8[:, b, :], score[:, ats[b]], TAKEN
                                                    ).then_inc(top_step, 1)

                def maxima(hh, bank):
                    g, h = divmod(hh, NH)
                    s = hh % 2
                    wait_apart(qk_mm, l * 2 * NH + (hh + 1))
                    for b, at, n in ((0, slice(0, P), P), (1, slice(P, S3), S)):
                        add = (bias[:, h, S - n:S] if g == 0 else cmask[:, S - n:S])
                        t = nc.vector.tensor_tensor_reduce(lg[:, s, at], ps[:, bank, at], add, 1.0, LOWEST,
                                                           ALU.add, ALU.max, mx[:, s, b:b + 1])
                    t.then_inc(lg_out, 1)
                    dve.wait_ge(lg_out, l * 2 * NH + (hh + 1))
                    if g == 0:
                        nc.vector.tensor_scalar(nm[:, s, :], mx[:, s, :], -SCALE, None, ALU.mult).then_inc(nm_out, 1)
                    else:
                        nc.vector.scalar_tensor_tensor(out=mt[:, s, :], in0=mx[:, s, :], scalar=SCALE,
                                                       in1=cumq[:, :, h], op0=ALU.mult, op1=ALU.add).then_inc(mt_out, 1)
                        dve.wait_ge(mt_out, l * NH + (h + 1))
                        nc.vector.tensor_tensor(nm[:, s, :], cumq[:, :, h], mt[:, s, :], ALU.subtract).then_inc(nm_out, 1)

                def turned(hh, bank):
                    dve.wait_ge(tr_mm, l * 2 * NH + (hh + 1))
                    nc.vector.tensor_copy(prT[:, hh % 2, :], ps[:, bank, 0:S3]).then_inc(prT_out, 1)

                def outputs(t, bank):
                    heads, g, half = slice(4 * t, 4 * t + 4), t // 2, t % 2
                    dve.wait_ge(pv_mm, l * 2 * NH + 4 * (t + 1))
                    nc.vector.reciprocal(rinv[:, :, heads], rsum[:, :, heads]).then_inc(rinv_out, 1)
                    dve.wait_ge(rinv_out, l * 4 + (t + 1))
                    for b in range(NB):
                        v = nc.vector.tensor_tensor(
                            xn[:, b, t * S:(t + 1) * S].rearrange("p (h d) -> p h d", h=4),
                            ps[:, bank, b * S:(b + 1) * S].rearrange("p (h d) -> p h d", h=4),
                            rinv[:, b, heads].unsqueeze(2).to_broadcast([P, 4, HD]), ALU.mult)
                    v.then_inc(o_out, 1)

                def out_low(t, bank):
                    dve.wait_ge(othi_out, l * 4 + (t + 1))
                    at = slice(2 * t, 2 * t + 2)
                    nc.vector.tensor_tensor(xlo[:, at, :].rearrange("p a t -> p (a t)"), ps[:, bank, :],
                                            xhi[:, at, :].rearrange("p a t -> p (a t)").bitcast(F32),
                                            ALU.subtract).then_inc(otlo_out, 1)

                def tile_out(j):
                    dve.wait_ge(feat_mm, l * NFEAT + j + 1)
                    nc.vector.tensor_tensor(feat[:, j, :], ps[:, GU + j % 2, 0:S], rows[:, :], ALU.mult
                                            ).then_inc(feat_out, 1)

                dve.wait_ge(table_out, 16)
                dve.wait_ge(const_in, 16)
                dve.wait_ge(c_mm, l + 1)
                nc.vector.tensor_tensor(ct, ps[:, CB, 0:S], rows[:, :], ALU.mult).then_inc(ct_out, 1)
                dve.wait_ge(feat_mm, l * NFEAT + KI + 1)
                nc.vector.tensor_copy(wft[:, :], ps[HD:KW, GU + KI, 0:S]).then_inc(wft_out, 1)
                for half in (slice(0, HD), slice(HD, P)):
                    t = nc.vector.tensor_tensor(feat[half, KI, :], ps[0:HD, GU + KI, 0:S], rows[0:HD, :], ALU.mult)
                t.then_inc(feat_out, 1)
                dve.wait_ge(wf_mm, l + 1)
                for b in range(NB):
                    at = b * 2 * NH
                    nc.vector.tensor_scalar(wf[:, b, :], ps[:, WFB, at:at + NH], rstd[:, b:b + 1], W_SCALE,
                                            ALU.mult, ALU.mult)
                    t = nc.vector.scalar_tensor_tensor(out=zf[:, b, :], in0=ps[:, WFB, at + NH:at + 2 * NH],
                                                       scalar=rstd[:, b:b + 1], in1=gain[:, G_BF:G_BF + NH],
                                                       op0=ALU.mult, op1=ALU.add)
                t.then_inc(z_out, 1)
                dve.wait_ge(z_out, l + 1)
                nc.vector.tensor_scalar(mz[:], zf[:], 0.0, None, ALU.min)
                nc.vector.scalar_tensor_tensor(out=az[:], in0=zf[:], scalar=-1.0, in1=zf[:], op0=ALU.mult,
                                               op1=ALU.max).then_inc(az_out, 1)
                dve.wait_ge(css_mm, l + 1)
                nc.vector.tensor_scalar(cms[:, :], ps[:, CB, 0:NB], 1.0 / P, EPS, ALU.mult, ALU.add).then_inc(cms_out, 1)
                back(1)
                tile_out(QI)
                dve.wait_ge(crstd_out, l + 1)
                for b in range(NB):
                    t = nc.vector.tensor_scalar(diag[:, b, :], ident, crstd[:, b:b + 1], None, ALU.mult)
                t.then_inc(cdiag_out, 1)
                dve.wait_ge(lz_out, l + 1)
                nc.vector.tensor_tensor(logf[:], mz[:], lz[:], ALU.subtract).then_inc(logf_out, 1)
                dve.wait_ge(crows_mm, l + 1)
                nc.vector.tensor_tensor(cn, ct, ps[:, CB, 0:S], ALU.mult).then_inc(cn_out, 1)
                front(2, (0,))
                tile_out(QI + 1)
                front(2, (1,))
                tile_out(QI + 2)
                back(2)
                dve.wait_ge(cum_mm, l + 1)
                for at, n in ((0, P), (P, S)):
                    t = nc.vector.tensor_scalar(ncum[:, at:at + n], ps[0:NH, SUM, 0:n], -1.0 / SCALE, None, ALU.mult)
                t.then_inc(ncum_out, 1)
                nc.vector.tensor_copy(cumq[:].rearrange("p b h -> p (b h)"),
                                      ps[:, SUM, CUMQ:CUMQ + NB * NH]).then_inc(cum_out, 1)
                dve.wait_ge(ncum_out, l + 1)
                nc.vector.tensor_copy(nchi[:], ncum[:]).then_inc(nchi_out, 1)
                dve.wait_ge(nchi_out, l + 1)
                nc.vector.tensor_tensor(nclo[:], ncum[:], nchi[:].bitcast(F32), ALU.subtract).then_inc(nclo_out, 1)
                dve.wait_ge(chi_out, l + 1)
                nc.vector.scalar_tensor_tensor(out=clo[:], in0=cn, scalar=gain[:, G_CKV:G_CKV + 1],
                                               in1=chi[:].bitcast(F32), op0=ALU.mult, op1=ALU.subtract
                                               ).then_inc(clo_out, 1)
                tile_out(QI + 3)
                for h in range(NH):
                    dve.wait_ge(relu_out, l * NH + (h + 1))
                    if h:
                        dve.wait_ge(score_out, l * NH + h)
                    for b, at, n in ((0, slice(0, P), P), (1, slice(P, S3), S)):
                        t = nc.vector.scalar_tensor_tensor(
                            out=score[:, at], in0=relu[:, h % 2, at], scalar=wf[:, b, h:h + 1],
                            in1=score[:, at] if h else cmask[:, S - n:S], op0=ALU.mult, op1=ALU.add)
                    t.then_inc(score_out, 1)
                nc.vector.tensor_copy(pickr[:], pick).then_inc(pickr_set, 1)
                front(3)
                take(0, 2)
                tile_out(QA)
                back(3)
                take(2, 3)
                tile_out(QA + 1)
                front(4, (0,))
                take(3, 4)
                tile_out(QA + 2)
                front(4, (1,))
                take(4, 5)
                back(4)
                tile_out(QA + 3)
                take(5, 6)
                front(5, (0,))
                tile_out(FX)
                take(6, 7)
                front(5, (1,))
                tile_out(FX + 1)
                take(7, 8)
                wait_apart(top_step, (l + 1) * (2 * NB * (TOPK // 8)))
                nc.vector.scalar_tensor_tensor(out=drop[:], in0=score[:], scalar=TAKEN, in1=noncausal,
                                               op0=ALU.not_equal, op1=ALU.max).then_inc(drop_out, 1)
                back(5)
                tile_out(FX + 2)
                front(6, (0,))
                front(6, (1,))
                tile_out(FX + 3)
                back(6)
                dve.wait_ge(bias_in, 16)
                for k in range(NH + 2):
                    if k < NH:
                        maxima(k, 6)
                    if k < 4:
                        tile_out(FX + 4 + k)
                    if 1 <= k <= NH:
                        turned(k - 1, 7)
                    if k == 1:
                        front(7)
                    if k == 2:
                        back(7)
                    if k == 4:
                        front(8)
                        back(8)
                    if k == 6:
                        front(9)
                        outputs(0, 0)
                    if k == 7:
                        back(9)
                for k in range(NH + 2):
                    if k < NH:
                        maxima(NH + k, 4)
                    if k == 0:
                        outputs(1, 1)
                        out_low(0, 0)
                    if 1 <= k <= NH:
                        turned(NH + k - 1, 5)
                    if k == 2:
                        out_low(1, 7)
                    if k == 1:
                        front(10)
                        back(10)
                    if k == 6:
                        outputs(2, 6)
                        front(11)
                    if k == 8:
                        out_low(2, 6)
                        back(11)
                outputs(3, 7)
                front(12)
                out_low(3, 7)
                back(12)
                dve.wait_ge(wo_mm, l * 2 * KT + (2 * KT - 1))
                residual(0, 0, 1.0)
                residual(0, 1, 1.0)
                dve.wait_ge(acc_mm, l * 5 + 3)
                residual(1, 0, 1.0)
                dve.wait_ge(wo_mm, l * 2 * KT + 2 * KT)
                residual(1, 1, 1.0)

            nc.vector.memset(ones[:], 1.0).then_inc(ones_set, 1)
            dve.wait_ge(rb_in, 16)
            dve.wait_ge(table_in, 16)
            rb_wide = rb.unsqueeze(2).to_broadcast([NBUCKET, NH, P])
            nc.vector.tensor_copy(rbhi, rb_wide).then_inc(rb_set, 1)
            nc.vector.tensor_copy(onehot_r, onehot).then_inc(rb_set, 1)
            dve.wait_ge(rb_set, 1)
            nc.vector.tensor_tensor(rblo, rb_wide, rbhi.bitcast(F32), ALU.subtract).then_inc(rb_set, 1)
            nc.vector.tensor_scalar(nident[:], ident, NEG, None, ALU.mult).then_inc(nident_set, 1)
            for b in range(NB):
                dve.wait_ge(x_in[b], 16)
                nc.vector.memset(spare[:, b:b + 1], 0.0).then_inc(x_ready, 2)
            with dve.Fori(0, DEPTH) as l:
                split_front(l, 0, halves=(0,))
                norm(l * 3, G_FFN1, l, 1, first=True)
                ffn(l, 0)
                norm(l * 3 + 1, G_MIX, l, NF + 1)
                mix(l)
                norm(l * 3 + 2, G_FFN2, l, NF + MIXC + 1)
                ffn(l, 1)
            mean(DEPTH * 3, 0)
            mean(DEPTH * 3, 1)
            dve.wait_ge(fgain_in, 16)
            for b in range(NB):
                dve.wait_ge(rstd_out, (DEPTH * 3) * NB + b + 1)
                nc.vector.scalar_tensor_tensor(out=xn[:, b, :], in0=X[:, b, :], scalar=rstd[:, b:b + 1], in1=fgain[:],
                                               op0=ALU.mult, op1=ALU.mult).then_inc(fin_out, 1)


def bucket(dist):
    dist, exact = max(dist, 0), NBUCKET // 2
    if dist < exact:
        return dist
    ratio = MAXDIST // exact
    steps = sum(dist ** exact >= exact ** exact * ratio ** k for k in range(1, exact + 1))
    return min(exact + steps, NBUCKET - 1)


def shape_constants():
    c = np.zeros((P, NC), np.float32)
    row, col = np.arange(P)[:, None], np.arange(P)[None, :]
    c[:, C_ID:C_ID + P] = row == col
    c[:, C_CM + P:C_CM + S] = np.where(col > row, np.float32(NEG), np.float32(0))
    c[:, C_NC:C_NC + P] = c[:, C_NC + 2 * P:C_NC + S3] = col > row
    for b in range(NB):
        c[:, C_U + b * S:C_U + (b + 1) * S] = b * P + row <= np.arange(S)[None, :]
    for h in range(NH):
        c[h, C_E + h * P:C_E + (h + 1) * P] = 1
    for y in range(TAB):
        c[bucket(2 * P - 1 - y), C_OH + y] = 1
    return c


def by_k(w, n):
    layers, k, cols = w.shape
    return w.reshape(layers, k // P, P, cols // n, n).transpose(0, 3, 2, 1, 4).reshape(layers, cols // n, P, -1)


def lay_out(a):
    f = np.float32
    stream = np.zeros((DEPTH, LC, P, CHUNK), f)
    for name, at in (("ffn1", 0), ("ffn2", NF + MIXC)):
        stream[:, at:at + NF, :, 0:UNIT] = by_k(a[name + "_gate"], P)
        stream[:, at:at + NF, :, UNIT:FRONT] = by_k(a[name + "_up"], P)
        stream[:, at:at + NF, :, FRONT:] = a[name + "_down"].reshape(DEPTH, NF, P, D)
    w = a["w_in"]
    hw = NH * HD
    at = np.cumsum([0, hw, P, NH * HD, HD, NH, hw, hw, hw, NH])
    qa, c, qi, ki, wi, fq, fk, fv, fl = (w[:, :, at[i]:at[i + 1]] for i in range(9))
    qa, qi, fq, fk = (by_k(t, P) for t in (qa, qi, fq, fk))
    fv = by_k(fv, hw)[:, 0]
    wo = a["w_out"].reshape(DEPTH, KT, P, D)
    place = {
        0: [np.concatenate([by_k(c, P)[:, 0], by_k(np.concatenate([ki, wi, fl], 2), KW)[:, 0]], 2)],
        1: [qi[:, 0], qi[:, 1], qi[:, 2]],
        2: [qi[:, 3], np.concatenate([a["w_uk"].reshape(DEPTH, P, hw), a["w_uv"].reshape(DEPTH, P, hw)], 2), qa[:, 0]],
        3: [qa[:, 1], qa[:, 2], qa[:, 3]],
        4: [fq[:, 0], fk[:, 0], fq[:, 1]],
        5: [fk[:, 1], fq[:, 2], fk[:, 2]],
        6: [fq[:, 3], fk[:, 3]],
        7: [fv[:, :, i * UNIT:(i + 1) * UNIT] for i in range(3)],
        8: [fv[:, :, 3 * UNIT:]],
        9: [wo[:, 0], wo[:, 1], wo[:, 2]],
        10: [wo[:, 3], wo[:, 4], wo[:, 5]],
        11: [wo[:, 6], None, wo[:, 7]],
    }
    for m, parts in place.items():
        for i, part in enumerate(parts):
            if part is not None:
                stream[:, NF + m, :, i * UNIT:i * UNIT + part.shape[2]] = part
    gains = np.zeros((P, DEPTH, NG), f)
    for name, col in (("ffn1_norm", G_FFN1), ("mix_norm", G_MIX), ("ffn2_norm", G_FFN2)):
        gains[:, :, col:col + KT] = a[name].reshape(DEPTH, KT, P).transpose(2, 0, 1)
    gains[:, :, G_CKV] = a["ckv_norm"].T
    gains[:, :, G_BF:] = a["b_forget"][None]
    return {
        "x": np.ascontiguousarray(a["x"].reshape(NB, P, D).transpose(1, 0, 2)),
        "stream": stream.reshape(NCHUNK, P, CHUNK),
        "gains": gains,
        "final_gain": np.ascontiguousarray(np.broadcast_to(a["final_norm"][None], (P, D))),
        "consts": shape_constants(),
        "rel_bias": np.ascontiguousarray(a["rel_bias"]),
    }


def kernel(**inputs):
    import concourse.bacc as bacc
    from concourse.bass_utils import run_bass_kernel_spmd

    arrays = lay_out({k: np.asarray(v) for k, v in inputs.items()})
    nc = bacc.Bacc("TRN2", target_bir_lowering=False, num_devices=1)
    args = [nc.dram_tensor(k, v.shape, F32, kind="ExternalInput").ap() for k, v in arrays.items()]
    out = nc.dram_tensor("out", (NB, P, D), F32, kind="ExternalOutput").ap()
    table = nc.dram_tensor("table", (NH, P * TAB), F32, kind="Internal").ap()
    trunk(nc, *args, out, table)
    r = run_bass_kernel_spmd(nc, [arrays], core_ids=[0])
    return r.results[0]["out"].reshape(1, S, D)
```

```python
from contextlib import ExitStack

import numpy as np

import concourse.bass as bass
from concourse import mybir

F32 = mybir.dt.float32
F32R = mybir.dt.float32r
BF16 = mybir.dt.bfloat16
ALU = mybir.AluOpType
ACT = mybir.ActivationFunctionType

P = 128
D = 1024
S = 256
S3 = 3 * P
DEPTH = 2
NB = S // P
KT = D // P
HD = 64
NH = 8
TOPK = S // 4
DFF = ((8 * D // 3 + P - 1) // P) * P
NF = DFF // P
NBUCKET = 32
MAXDIST = 128
EPS = 1e-6
NEG = -1e30
TAKEN = -3e38
LOWEST = -3.4e38
SCALE = HD ** -0.5
W_SCALE = NH ** -0.5

UNIT = 1024
FRONT = 2 * UNIT
CHUNK = 3 * UNIT
MIXC = 12
LC = 2 * NF + MIXC
NCHUNK = DEPTH * LC
TAB = 384
TINY = 8
LO = 64
KW = HD + 2 * NH

MIX_USED = [(KT * (P + KW), TINY), (FRONT, UNIT), (FRONT, UNIT), (FRONT, UNIT), (FRONT, UNIT), (FRONT, UNIT),
            (FRONT, TINY), (FRONT, UNIT), (UNIT, TINY), (FRONT, UNIT), (FRONT, UNIT), (UNIT, UNIT)]

KI, QI, KA, QA, FX = 0, 1, 5, 9, 13
NFEAT = 21
NQI = KA - QI
NTILE = 1 + NFEAT - QA

G_FFN1, G_MIX, G_FFN2, G_CKV, G_BF = 0, KT, 2 * KT, 3 * KT, 3 * KT + 1
NG = G_BF + NH
C_ID = 0
C_OH = C_ID + P
C_RB = C_OH + TAB
C_CM = C_RB + NH
C_NC = C_CM + S
C_U = C_NC + S3
C_E = C_U + NB * S
NC = C_E + NH * P


def trunk(nc, x, stream, gains, final_gain, consts, rel_bias, out, table):
    with ExitStack() as ctx:
        def sb(name, shape, dt=F32):
            return ctx.enter_context(nc.sbuf_tensor(name, shape, dt))

        def sems(names):
            return [ctx.enter_context(nc.semaphore(n)) for n in names.split()]

        raw = sb("raw", [P, 2, CHUNK])
        whi = sb("whi", [P, 2, CHUNK], F32R)
        wlo = sb("wlo", [P, 2, CHUNK], F32R)
        X = sb("X", [P, NB, D])
        xn = sb("xn", [P, NB, D])
        xhi = sb("xhi", [P, KT, S], F32R)
        xlo = sb("xlo", [P, KT, S], F32R)
        ones = sb("ones", [P, P])
        diag = sb("diag", [P, NB, P])
        rows = sb("rows", [P, S])
        pickr = sb("pickr", [LO + NH, NH, P], F32R)
        nc2 = sb("nc2", [LO + NH, S3], F32R)
        ss = sb("ss", [P, NB])
        ms = sb("ms", [P, NB])
        rstd = sb("rstd", [P, NB])
        mhalf = sb("mhalf", [P, NB])
        gains_all = sb("gains_all", [P, DEPTH, NG])
        gain = sb("gain", [P, NG])
        fgain = sb("fgain", [P, D])
        hg = sb("hg", [P, 2, S])
        ur = sb("ur", [P, 2, S])
        sig = sb("sig", [P, 2, S])
        ht = sb("ht", [P, 2, S])
        hf = sb("hf", [P, 2, S])
        hhi = sb("hhi", [P, 2, S], F32R)
        hlo = sb("hlo", [P, 2, S], F32R)
        cst = sb("cst", [P, NC])
        nident = sb("nident", [P, P], BF16)
        bias = sb("bias", [P, NH, S])
        feat = sb("feat", [P, NFEAT, S])
        val = sb("val", [P, NB, D])
        wft = sb("wft", [2 * NH, S])
        wf = sb("wf", [P, NB, NH])
        zf = sb("zf", [P, NB, NH])
        az = sb("az", [P, NB, NH])
        mz = sb("mz", [P, NB, NH])
        ez = sb("ez", [P, NB, NH])
        lz = sb("lz", [P, NB, NH])
        logf = sb("logf", [P, NB, NH])
        cumq = sb("cumq", [P, NB, NH])
        cms = sb("cms", [P, NB])
        crstd = sb("crstd", [P, NB])
        chi = sb("chi", [P, S], F32R)
        clo = sb("clo", [P, S], F32R)
        relu = sb("relu", [P, 2, S3])
        score = sb("score", [P, S3])
        top8 = sb("top8", [P, NB, 8])
        drop = sb("drop", [P, S3], BF16)
        lg = sb("lg", [P, 2, S3])
        mx = sb("mx", [P, 2, NB])
        mt = sb("mt", [P, 2, NB])
        nm = sb("nm", [P, 2, NB])
        ct, csq, cn = (t[:, 0, :] for t in (hg, sig, hf))
        pr = sb("pr", [P, 2, S3])
        prT = sb("prT", [P, 2, S3])
        rsum = sb("rsum", [P, NB, 2 * NH])
        rinv = sb("rinv", [P, NB, 2 * NH])
        warm = sb("warm", [P, NB])
        spare = sb("spare", [P, 2 * NB])

        ident = cst[:, C_ID:C_ID + P]
        cmask = cst[:, C_CM:C_CM + S]
        noncausal = cst[:, C_NC:C_NC + S3]
        tri = cst[:, C_U:C_U + NB * S].rearrange("p (b t) -> p b t", b=NB)
        pick = cst[0:LO + NH, C_E:C_E + NH * P].rearrange("p (h q) -> p h q", h=NH)
        onehot = cst[0:NBUCKET, C_OH:C_OH + TAB]
        rb = cst[0:NBUCKET, C_RB:C_RB + NH]
        rbhi, rblo = (wlo[0:NBUCKET, 1, i * NH * P:(i + 1) * NH * P].rearrange("p (h q) -> p h q", h=NH)
                      for i in range(2))
        onehot_r = wlo[0:NBUCKET, 1, FRONT:FRONT + TAB]
        tab = feat[:, 0:12, :].rearrange("p a t -> p (a t)").rearrange("p (h y) -> p h y", h=NH)

        ps = ctx.enter_context(nc.psum_tensor("ps", [P, 8, 512], F32))
        GU = 4
        LASTUP = 7
        ROWS = 7
        CB = 2
        KIB = 0
        WFB = 3
        SUM, CUMQ = 1, S

        front_in, back_in = sems("front_in0 front_in1"), sems("back_in0 back_in1")
        x_in = sems("x_in0 x_in1")
        table_in, const_in, rb_in, gain_in, fgain_in = sems("table_in const_in rb_in gain_in fgain_in")
        table_out, bias_in, out_done = sems("table_out bias_in out_done")
        half_set, nident_set, rb_set, gain_set, tab_mm, tab_sb = sems(
            "half_set nident_set rb_set gain_set tab_mm tab_sb")
        hi_front, hi_back = sems("hi_front hi_back")
        w_front, w_back = sems("w_front w_back")
        front_done, back_done = sems("front_done back_done")
        x_ready, ss_out, ms_out, rstd_out, diag_out, rows_mm, rows_out = sems(
            "x_ready ss_out ms_out rstd_out diag_out rows_mm rows_out")
        ones_set, nc2_set, pickr_set, ur_out, ht_out, nchi_out = sems(
            "ones_set nc2_set pickr_set ur_out ht_out nchi_out")
        xt_mm, xhi_out, xlo_out = sems("xt_mm xhi_out xlo_out")
        (gate_mm,) = sems("gate_mm")
        sig_out, hg_out, h_out, hhi_out, hlo_out, acc_mm = sems("sig_out hg_out h_out hhi_out hlo_out acc_mm")
        feat_mm, feat_out, ka_out, qi_out, wo_mm = sems("feat_mm feat_out ka_out qi_out wo_mm")
        nclo_out, z_out, az_out, ez_out, lz_out, logf_out = sems("nclo_out z_out az_out ez_out lz_out logf_out")
        cum_mm, cum_out = sems("cum_mm cum_out")
        c_mm, ct_out, csq_out, css_mm, cms_out, crstd_out, cdiag_out, crows_mm = sems(
            "c_mm ct_out csq_out css_mm cms_out crstd_out cdiag_out crows_mm")
        wft_out, wf_mm, cn_out, chi_out, clo_out = sems("wft_out wf_mm cn_out chi_out clo_out")
        idx_mm, relu_out, score_out, top_step, drop_out = sems("idx_mm relu_out score_out top_step drop_out")
        va_mm, va_out, vf_mm, vf_out = sems("va_mm va_out vf_mm vf_out")
        qk_mm, lg_out, mt_out, nm_out, pr_out = sems("qk_mm lg_out mt_out nm_out pr_out")
        tr_mm, prT_out, pv_mm = sems("tr_mm prT_out pv_mm")
        rinv_out, o_out, ot_mm, othi_out, otlo_out = sems("rinv_out o_out ot_mm othi_out otlo_out")
        (fin_out,) = sems("fin_out")

        def chunk(l, k, i=0):
            return l * LC + i * 2 + k

        def arrivals(l, k, i=0):
            return (l * (LC // 2) + i + (k // 2 + 1)) * 16

        block = ctx.enter_context(nc.Block())

        @block.sync
        def _(sp):
            sp.dma_start(cst[:, 0:C_RB], consts[:, 0:C_RB]).then_inc(table_in, 16)
            sp.dma_start(rb, rel_bias).then_inc(rb_in, 16)
            for b in range(NB):
                sp.dma_start(X[:, b, :], x[:, b, :]).then_inc(x_in[b], 16)
            sp.dma_start(gains_all[:, :, :], gains).then_inc(gain_in, 16)

            def load_front(s, i):
                sp.dma_start(raw[:, s, 0:FRONT], stream[bass.ds(i * 2 + s, 1), :, 0:FRONT].rearrange(
                    "a p n -> (a p) n")).then_inc(front_in[s], 16)

            def load_back(s, i):
                sp.dma_start(raw[:, s, FRONT:CHUNK], stream[bass.ds(i * 2 + s, 1), :, FRONT:CHUNK].rearrange(
                    "a p n -> (a p) n")).then_inc(back_in[s], 16)

            def reload(i):
                for s in range(2):
                    sp.wait_ge(w_front, (i * 2 + s - 1) * 2)
                    load_front(s, i)
                    sp.wait_ge(w_back, i * 2 + s - 1)
                    load_back(s, i)

            for s in range(2):
                load_front(s, 0)
                load_back(s, 0)
            sp.dma_start(cst[:, C_CM:NC], consts[:, C_CM:NC]).then_inc(const_in, 16)
            sp.wait_ge(tab_sb, NH)
            sp.dma_start(table.rearrange("h (p y) -> p h y", y=TAB), tab).then_inc(table_out, 16)
            reload(1)
            sp.wait_ge(table_out, 16)
            skew = table[:, P - 1:P - 1 + P * (TAB - 1)].rearrange("h (p y) -> p h y", y=TAB - 1)
            sp.dma_start(bias[:, :, :], skew[:, :, 0:S]).then_inc(bias_in, 16)
            sp.dma_start(fgain[:, :], final_gain).then_inc(fgain_in, 16)
            with sp.Fori(2, NCHUNK // 2) as i:
                reload(i)
            for b in range(NB):
                for j in range(2):
                    at = slice(j * 512, (j + 1) * 512)
                    sp.wait_ge(fin_out, 2 * b + j + 1)
                    sp.dma_start(out[b, :, at], xn[:, b, at]).then_inc(out_done, 16)
            sp.wait_ge(out_done, 16 * NB * 2)

        @block.gpsimd
        def _(pool):
            nc.gpsimd.memset(mhalf[:], -0.5).then_inc(half_set, 1)
            pool.wait_ge(half_set, 1)

            def power(n):
                for b in range(NB):
                    pool.wait_ge(ms_out, n * NB + b + 1)
                    nc.gpsimd.tensor_tensor(rstd[:, b:b + 1], ms[:, b:b + 1], mhalf[:, b:b + 1],
                                            ALU.pow).then_inc(rstd_out, 1)

            with pool.Fori(0, DEPTH) as l:
                power(l * 3)
                pool.wait_ge(const_in, 16)
                nc.gpsimd.tensor_copy(pickr[:], pick).then_inc(pickr_set, 1)
                power(l * 3 + 1)
                pool.wait_ge(cms_out, l + 1)
                nc.gpsimd.tensor_tensor(crstd[:, :], cms[:, :], mhalf[:, :], ALU.pow).then_inc(crstd_out, 1)
                power(l * 3 + 2)
            power(DEPTH * 3)

        @block.scalar
        def _(act):
            def split_front(l, k, i=0, used=FRONT):
                act.wait_ge(front_in[k % 2], arrivals(l, k, i))
                for at in (slice(0, used // 2), slice(used // 2, used)):
                    nc.scalar.copy(whi[:, k % 2, at], raw[:, k % 2, at]).then_inc(hi_front, 1)

            def split_back(l, k, i=0, used=UNIT):
                act.wait_ge(back_in[k % 2], arrivals(l, k, i))
                nc.scalar.copy(whi[:, k % 2, FRONT:FRONT + used],
                               raw[:, k % 2, FRONT:FRONT + used]).then_inc(hi_back, 1)

            def squares(n, b):
                act.wait_ge(x_ready, n * (2 * NB) + (2 * b + 2))
                nc.scalar.activation(xn[:, b, :], X[:, b, :], ACT.Square,
                                     accum_out=ss[:, b:b + 1]).then_inc(ss_out, 1)

            def norm(n, g, l, ahead=None):
                squares(n, 0)
                for k in range(KT):
                    if k % 2 == 0:
                        act.wait_ge(xt_mm, n * (KT // 2) + (k // 2 + 1))
                    nc.scalar.mul(xhi[:, k, :], ps[:, 4 + k // 2, S * (k % 2):S * (k % 2) + S],
                                  gain[:, g + k:g + k + 1]).then_inc(xhi_out, 1)
                if ahead is not None:
                    split_front(l, ahead)
                squares(n, 1)

            def ffn(l, phase):
                k0 = phase * (NF + MIXC)

                def step(f, i=0, back=UNIT, front=FRONT):
                    s, n = f % 2, l * (2 * NF) + i * 2 + (phase * NF + f)
                    act.wait_ge(hg_out, n + 1)
                    nc.scalar.activation(sig[:, s, :], hg[:, s, :], ACT.Sigmoid).then_inc(sig_out, 1)
                    act.wait_ge(h_out, n + 1)
                    nc.scalar.copy(hhi[:, s, :], hf[:, s, :]).then_inc(hhi_out, 1)
                    if back:
                        if f > 0:
                            act.wait_ge(back_done, n)
                        split_back(l, k0 + f + 1, i, back)
                    if front:
                        act.wait_ge(front_done, n + 1)
                        split_front(l, k0 + f + 2, i, front)

                step(0)
                step(1)
                with act.Fori(0, NF // 2 - 2) as i:
                    step(2, i)
                    step(3, i)
                step(NF - 2, front=MIX_USED[0][0] if phase == 0 else 0)
                step(NF - 1, back=MIX_USED[0][1] if phase == 0 else 0, front=MIX_USED[1][0] if phase == 0 else 0)

            def mix(l):
                def front(m):
                    split_front(l, NF + m, used=MIX_USED[m][0] if m < MIXC else FRONT)

                def back(m):
                    split_back(l, NF + m, used=MIX_USED[m][1] if m < MIXC else UNIT)

                def probs(hh):
                    act.wait_ge(nm_out, l * 2 * NH + hh + 1)
                    s = hh % 2
                    nc.scalar.activation(pr[:, s, 0:P], lg[:, s, 0:P], ACT.Exp, bias=nm[:, s, 0:1],
                                         scale=SCALE, accum_out=rsum[:, 0, hh:hh + 1])
                    nc.scalar.activation(pr[:, s, P:S3], lg[:, s, P:S3], ACT.Exp, bias=nm[:, s, 1:2],
                                         scale=SCALE, accum_out=rsum[:, 1, hh:hh + 1]).then_inc(pr_out, 1)

                def out_high(t, bank):
                    act.wait_ge(ot_mm, l * 4 + t + 1)
                    nc.scalar.copy(xhi[:, 2 * t:2 * t + 2, :].rearrange("p a t -> p (a t)"),
                                   ps[:, bank, :]).then_inc(othi_out, 1)

                def query_out(j):
                    act.wait_ge(feat_mm, l * NFEAT + j + 1)
                    nc.scalar.copy(feat[:, j, :], ps[:, GU + j % 2, 0:S]).then_inc(qi_out, 1)

                back(1)
                act.wait_ge(ct_out, l + 1)
                nc.scalar.activation(csq, ct, ACT.Square).then_inc(csq_out, 1)
                act.wait_ge(table_out, 16)
                query_out(QI)
                act.wait_ge(az_out, l + 1)
                nc.scalar.activation(ez[:], az[:], ACT.Exp, scale=-1.0).then_inc(ez_out, 1)
                act.wait_ge(ez_out, l + 1)
                nc.scalar.activation(lz[:], ez[:], ACT.Ln, bias=1.0).then_inc(lz_out, 1)
                act.wait_ge(c_mm, l + 1)
                front(2)
                act.wait_ge(feat_mm, l * NFEAT + (KI + 1))
                back(2)
                query_out(QI + 1)
                act.wait_ge(cum_mm, l + 1)
                for at, n in ((0, P), (P, S)):
                    t = nc.scalar.mul(nc2[0:NH, at:at + n], ps[0:NH, SUM, 0:n], -1.0 / SCALE)
                t.then_inc(nchi_out, 1)
                act.wait_ge(cn_out, l + 1)
                nc.scalar.mul(chi[:, :], cn, gain[:, G_CKV:G_CKV + 1]).then_inc(chi_out, 1)
                query_out(QI + 2)
                front(3)
                query_out(QI + 3)
                for h in range(NH):
                    act.wait_ge(idx_mm, l * NH + h + 1)
                    if h >= 2:
                        act.wait_ge(score_out, l * NH + h - 1)
                    nc.scalar.activation(relu[:, h % 2, :], ps[:, 6 + h % 2, 0:S3], ACT.Relu,
                                         scale=SCALE * W_SCALE).then_inc(relu_out, 1)
                    if 2 <= h < 2 + (QA - KA):
                        j = KA + h - 2
                        act.wait_ge(feat_mm, l * NFEAT + j + 1)
                        nc.scalar.copy(feat[:, j, :], ps[:, GU + j % 2, 0:S]).then_inc(ka_out, 1)
                act.wait_ge(va_mm, l + 1)
                for b in range(NB):
                    nc.scalar.copy(val[:, b, 0:D // 2], ps[:, b, :]).then_inc(va_out, 1)
                back(3)
                front(4)
                act.wait_ge(feat_mm, l * NFEAT + (QA + 1))
                back(4)
                act.wait_ge(feat_mm, l * NFEAT + (QA + 3))
                front(5)
                act.wait_ge(feat_mm, l * NFEAT + (QA + 4))
                back(5)
                act.wait_ge(feat_mm, l * NFEAT + (FX + 2))
                front(6)
                act.wait_ge(feat_mm, l * NFEAT + (FX + 3))
                back(6)
                for k in range(2 * NH + 2):
                    if k == 1:
                        act.wait_ge(feat_mm, l * NFEAT + (FX + 5))
                        front(7)
                    if k == 2:
                        act.wait_ge(feat_mm, l * NFEAT + (FX + 6))
                        back(7)
                    if k == 4:
                        act.wait_ge(feat_mm, l * NFEAT + NFEAT)
                        front(8)
                        back(8)
                    if k == 6:
                        act.wait_ge(vf_mm, l * 4 + 2)
                        front(9)
                    if k == 7:
                        act.wait_ge(vf_mm, l * 4 + 3)
                        back(9)
                    if k == NH:
                        out_high(0, 0)
                        act.wait_ge(vf_mm, l * 4 + 4)
                        for b in range(NB):
                            nc.scalar.mul(val[:, b, D // 2:D], ps[:, 2 + b, :], rstd[:, b:b + 1]).then_inc(vf_out, 1)
                    if k < 2 * NH:
                        probs(k)
                    if k == NH:
                        front(10)
                    if k == NH + 1:
                        back(10)
                    if k == NH + 3:
                        out_high(1, 7)
                    if k == NH + 6:
                        act.wait_ge(wo_mm, l * 2 * KT + 4)
                        front(11)
                    if k == NH + 7:
                        out_high(2, 6)
                    if k == NH + 8:
                        act.wait_ge(wo_mm, l * 2 * KT + 6)
                        back(11)
                out_high(3, 7)
                act.wait_ge(wo_mm, l * 2 * KT + 10)
                front(12)
                act.wait_ge(wo_mm, l * 2 * KT + 12)
                back(12)
                act.wait_ge(wo_mm, l * 2 * KT + 14)
                front(13)

            act.wait_ge(half_set, 1)
            nc.scalar.activation(warm[:], mhalf[:, 0:NB], ACT.Sigmoid)
            for h in range(NH):
                act.wait_ge(tab_mm, h + 1)
                nc.scalar.mul(tab[:, h, :], ps[:, h % 4, 0:TAB], 1.0 / SCALE).then_inc(tab_sb, 1)
            act.wait_ge(gain_in, 16)
            with act.Fori(0, DEPTH) as l:
                split_front(l, 0)
                act.wait_ge(x_ready, l * (3 * 2 * NB) + 1)
                nc.scalar.copy(gain[:, :], gains_all[:, bass.ds(l, 1), :].rearrange("p a n -> p (a n)")
                               ).then_inc(gain_set, 1)
                act.wait_ge(gain_set, l + 1)
                norm(l * 3, G_FFN1, l, 1)
                split_back(l, 0)
                ffn(l, 0)
                norm(l * 3 + 1, G_MIX, l)
                mix(l)
                norm(l * 3 + 2, G_FFN2, l)
                ffn(l, 1)
            for b in range(NB):
                squares(DEPTH * 3, b)

        @block.tensor
        def _(pe):
            def three(out_, a, b, start, stop):
                nc.tensor.matmul(out_, a[0], b[0], start=start, stop=False)
                nc.tensor.matmul(out_, a[0], b[1], start=False, stop=False)
                return nc.tensor.matmul(out_, a[1], b[0], start=False, stop=stop)

            def first(pairs, n):
                for k in range(KT):
                    pe.wait_ge(xhi_out, n + k + 1)
                    for out_, a in pairs:
                        nc.tensor.matmul(out_, a(k)[0], xhi[:, k, :], start=k == 0, stop=False)
                        nc.tensor.matmul(out_, a(k)[1], xhi[:, k, :], start=False, stop=False)
                for k in range(KT):
                    pe.wait_ge(xlo_out, n + k + 1)
                    last = [nc.tensor.matmul(out_, a(k)[0], xlo[:, k, :], start=False, stop=k == KT - 1)
                            for out_, a in pairs]
                return last

            def w(s, at, n):
                return whi[:, s, at:at + n], wlo[:, s, at:at + n]

            def xt(k, b=None):
                at = slice(0, S) if b is None else slice(b * P, (b + 1) * P)
                return xhi[:, k, at], xlo[:, k, at]

            def front_here(l, k, i=0, half=1):
                pe.wait_ge(w_front, chunk(l, k, i) * 2 + (half + 1))

            def back_here(l, k, i=0):
                pe.wait_ge(w_back, chunk(l, k, i) + 1)

            def norm(n):
                for b in range(NB):
                    for k in range(KT):
                        if k % 4 == 0:
                            pe.wait_ge(x_ready, n * (2 * NB) + (2 * b + k // 4 + 1))
                        t = nc.tensor.transpose(ps[:, 4 + k // 2, S * (k % 2) + b * P:S * (k % 2) + (b + 1) * P],
                                                X[:, b, k * P:(k + 1) * P], ident)
                        if b == NB - 1 and k % 2 == 1:
                            t.then_inc(xt_mm, 1)

            def spread(bank):
                for b in range(NB):
                    t = nc.tensor.matmul(ps[:, bank, b * P:(b + 1) * P], ones[:, :], diag[:, b, :], start=True, stop=True)
                return t

            def spread_rows(n):
                pe.wait_ge(diag_out, n + 1)
                spread(ROWS).then_inc(rows_mm, 1)

            def ffn(l, phase):
                k0 = phase * (NF + MIXC)

                def up(f, i=0):
                    s, n = f % 2, l * (2 * NF) + i * 2 + (phase * NF + f)
                    if f == 0:
                        front_here(l, k0)
                        first([(ps[:, g, 0:S], lambda k, g=g: w(0, g * UNIT + k * P, P)) for g in range(2)],
                              l * (3 * KT) + 2 * phase * KT)[1].then_inc(front_done, 1)
                        return
                    if f >= 3:
                        pe.wait_ge(ur_out, n - 1)
                    for g in range(2):
                        front_here(l, k0 + f, i, g)
                        to = ps[:, GU + s, g * S:(g + 1) * S]
                        if f == NF - 1 and g == 1:
                            to = ps[:, LASTUP, 0:S]
                        for k in range(KT):
                            if f == 1 and g == 0 and k == KT // 2:
                                spread_rows(l * 3 + 2 * phase)
                            t = three(to, w(s, g * UNIT + k * P, P), xt(k), k == 0, k == KT - 1)
                        if f == NF - 1 and g == 0:
                            t.then_inc(gate_mm, 1)
                    t.then_inc(front_done, 1)

                def down(f, i=0):
                    s, n = f % 2, l * (2 * NF) + i * 2 + (phase * NF + f)
                    back_here(l, k0 + f, i)
                    pe.wait_ge(hlo_out, n + 1)
                    for b in range(NB):
                        h = (hhi[:, s, b * P:(b + 1) * P], hlo[:, s, b * P:(b + 1) * P])
                        for j in range(2):
                            t = three(ps[:, 2 * b + j, :], h, w(s, FRONT + j * 512, 512), f == 0, f == NF - 1)
                            if f == NF - 1 and (b, j) in ((0, 1), (1, 0)):
                                t.then_inc(acc_mm, 1)
                    t.then_inc(back_done, 1)

                up(0)
                up(1)
                down(0)
                with pe.Fori(0, NF // 2 - 2) as i:
                    up(2, i)
                    down(1, i)
                    up(3, i)
                    down(2, i)
                up(NF - 2)
                down(NF - 3)
                up(NF - 1)
                down(NF - 2)
                down(NF - 1)

            def mix(l):
                def front(m, half=1):
                    front_here(l, NF + m, 0, half)
                    return m % 2

                def back(m):
                    back_here(l, NF + m)
                    return m % 2

                def tile(j, s, at, midway=None):
                    if QI + 2 <= j < QA:
                        pe.wait_ge(qi_out, l * NQI + (j - 2))
                    elif QA <= j < QA + 2:
                        pe.wait_ge(ka_out, l * (QA - KA) + (j - QA + 3))
                    elif j >= QA + 2:
                        pe.wait_ge(feat_out, l * NTILE + (j - QA))
                    for k in range(KT):
                        if midway and k == KT // 2:
                            midway()
                        t = three(ps[:, GU + j % 2, 0:S], w(s, at + k * P, P), xt(k), k == 0, k == KT - 1)
                    t.then_inc(feat_mm, 1)

                def value(u, s, at):
                    for b in range(NB):
                        for kk in range(2):
                            t = three(ps[:, 2 + b, :], xt(2 * u + kk, b), w(s, at + kk * 512, 512),
                                      2 * u + kk == 0, 2 * u + kk == KT - 1)
                    t.then_inc(vf_mm, 1)

                def project(k, b, s, at):
                    for j in range(2):
                        t = three(ps[:, 2 * b + j, :], xt(k, b), w(s, at + j * 512, 512), k == 0, k == KT - 1)
                        if (k, b, j) == (KT - 1, 1, 0):
                            t.then_inc(acc_mm, 1)
                    t.then_inc(wo_mm, 1)

                def logits(hh, bank):
                    g, h = divmod(hh, NH)
                    q, key = (QA + h // 2, KA + h // 2) if g == 0 else (FX + h // 2 * 2, FX + h // 2 * 2 + 1)
                    rows = slice(HD * (h % 2), HD * (h % 2) + HD)
                    if g == 0:
                        nc.tensor.matmul(ps[:, bank, 0:S3], nident[:], drop[:], start=True, stop=True)
                    else:
                        nc.tensor.matmul(ps[:, bank, 0:S3], pickr[:, h, :], nc2[:, :], start=True, stop=True)
                    nc.tensor.matmul(ps[:, bank, 0:P], feat[rows, q, 0:P], feat[rows, key, 0:P],
                                     start=False, stop=True, skip_group_check=True)
                    nc.tensor.matmul(ps[:, bank, P:S3], feat[rows, q, P:S], feat[rows, key, :],
                                     start=False, stop=True, skip_group_check=True).then_inc(qk_mm, 1)

                def turn(hh, bank):
                    pe.wait_ge(pr_out, l * 2 * NH + (hh + 1))
                    for j in range(3):
                        t = nc.tensor.transpose(ps[:, bank, j * P:(j + 1) * P], pr[:, hh % 2, j * P:(j + 1) * P], ident)
                    t.then_inc(tr_mm, 1)

                def attend(hh, bank):
                    pe.wait_ge(prT_out, l * 2 * NH + (hh + 1))
                    v, at, o = slice(hh * HD, (hh + 1) * HD), hh % 4 * HD, ps[:, bank + hh % NH // 4, :]
                    nc.tensor.matmul(o[:, at:at + HD], prT[:, hh % 2, 0:P], val[:, 0, v], start=True, stop=True)
                    nc.tensor.matmul(o[:, S + at:S + at + HD], prT[:, hh % 2, P:2 * P], val[:, 0, v], start=True, stop=False)
                    nc.tensor.matmul(o[:, S + at:S + at + HD], prT[:, hh % 2, 2 * P:S3], val[:, 1, v],
                                     start=False, stop=True).then_inc(pv_mm, 1)

                def turn_outputs(t2, bank):
                    pe.wait_ge(o_out, l * 4 + (t2 + 1))
                    for k in range(2):
                        for b in range(NB):
                            at = (2 * t2 + k) * P
                            t = nc.tensor.transpose(ps[:, bank, k * S + b * P:k * S + (b + 1) * P],
                                                    xn[:, b, at:at + P], ident)
                    t.then_inc(ot_mm, 1)

                def token_major():
                    pe.wait_ge(wft_out, l + 1)
                    for b in range(NB):
                        t = nc.tensor.matmul(ps[:, WFB, b * 2 * NH:(b + 1) * 2 * NH], wft[:, b * P:(b + 1) * P],
                                             ident[0:2 * NH, 0:2 * NH], start=True, stop=True)
                    t.then_inc(wf_mm, 1)
                    pe.wait_ge(csq_out, l + 1)
                    for b in range(NB):
                        t = nc.tensor.matmul(ps[:, CB, b:b + 1], csq[:, b * P:(b + 1) * P], ones[:, 0:1],
                                             start=True, stop=True)
                    t.then_inc(css_mm, 1)

                def latent_rows():
                    pe.wait_ge(cdiag_out, l + 1)
                    spread(CB).then_inc(crows_mm, 1)

                s = front(0)
                t, u = first([(ps[:, CB, 0:S], lambda k: w(0, k * P, P)),
                              (ps[0:KW, KIB, 0:S], lambda k: w(0, KT * P + k * KW, KW))], l * (3 * KT) + KT)
                t.then_inc(c_mm, 1)
                u.then_inc(feat_mm, 1)
                tile(QI, front(1, 0), 0, lambda: spread_rows(l * 3 + 1))
                tile(QI + 1, front(1), UNIT, token_major)
                tile(QI + 2, back(1), FRONT, latent_rows)
                pe.wait_ge(logf_out, l + 1)
                for b in range(NB):
                    nc.tensor.matmul(ps[0:NH, SUM, 0:S], logf[:, b, :], tri[:, b, :], start=b == 0, stop=b == 1)
                for b in range(NB):
                    for r in range(b + 1):
                        t = nc.tensor.matmul(ps[:, SUM, CUMQ + b * NH:CUMQ + (b + 1) * NH], tri[:, r, b * P:(b + 1) * P],
                                             logf[:, r, :], start=r == 0, stop=r == b)
                t.then_inc(cum_mm, 1)
                s = front(2)
                tile(QI + 3, s, 0)
                for h in range(NH):
                    if h == 0:
                        pe.wait_ge(feat_out, l * NTILE + 1)
                    if h % 2 == 0:
                        pe.wait_ge(qi_out, l * NQI + (h // 2 + 1))
                    if h >= 2:
                        pe.wait_ge(relu_out, l * NH + (h - 1))
                    rows_ = slice(HD * (h % 2), HD * (h % 2) + HD)
                    nc.tensor.matmul(ps[:, 6 + h % 2, 0:P], feat[rows_, QI + h // 2, 0:P], feat[rows_, KI, 0:P],
                                     start=True, stop=True)
                    nc.tensor.matmul(ps[:, 6 + h % 2, P:S3], feat[rows_, QI + h // 2, P:S], feat[rows_, KI, :],
                                     start=True, stop=True).then_inc(idx_mm, 1)
                    if 2 <= h < 2 + (QA - KA):
                        j = KA + h - 2
                        if h == 2:
                            pe.wait_ge(clo_out, l + 1)
                        if j < KA + 2:
                            pe.wait_ge(qi_out, l * NQI + (j - 2))
                        else:
                            pe.wait_ge(ka_out, l * (QA - KA) + (j - KA - 1))
                        three(ps[:, GU + j % 2, 0:S], w(s, UNIT + (j - KA) * P, P), (chi[:, :], clo[:, :]),
                              True, True).then_inc(feat_mm, 1)
                pe.wait_ge(cum_out, l + 1)
                for b in range(NB):
                    t = three(ps[:, b, :], (chi[:, b * P:(b + 1) * P], clo[:, b * P:(b + 1) * P]),
                              w(s, UNIT + 512, 512), True, True)
                t.then_inc(va_mm, 1)
                s = back(2)
                tile(QA, s, FRONT)
                tile(QA + 1, front(3, 0), 0)
                tile(QA + 2, front(3), UNIT)
                s = back(3)
                tile(QA + 3, s, FRONT)
                tile(FX, front(4, 0), 0)
                tile(FX + 1, front(4), UNIT)
                s = back(4)
                tile(FX + 2, s, FRONT)
                tile(FX + 3, front(5, 0), 0)
                pe.wait_ge(nident_set, 1)
                pe.wait_ge(drop_out, l + 1)
                pe.wait_ge(relu_out, l * NH + NH)
                pe.wait_ge(va_out, l * NB + NB)
                pe.wait_ge(ka_out, (l + 1) * (QA - KA))
                pe.wait_ge(feat_out, l * NTILE + (1 + FX - QA))
                for k in range(2 * NH + 2):
                    if k < 2 * NH:
                        if k == NH:
                            pe.wait_ge(pickr_set, l + 1)
                            pe.wait_ge(nclo_out, l + 1)
                            pe.wait_ge(feat_out, l * NTILE + NTILE)
                        elif k >= 1:
                            pe.wait_ge(lg_out, l * 2 * NH + k)
                        logits(k, 6 if k < NH else 4)
                    if k == 0:
                        tile(FX + 4, front(5), UNIT)
                    elif k == 1:
                        tile(FX + 5, back(5), FRONT)
                    elif k == 2:
                        tile(FX + 6, front(6, 0), 0)
                    elif k == 3:
                        tile(FX + 7, front(6), UNIT)
                    elif k == 4:
                        value(0, front(7, 0), 0)
                    elif k == 5:
                        value(1, front(7), UNIT)
                    elif k == 6:
                        value(2, back(7), FRONT)
                    elif k == 7:
                        value(3, front(8), 0)
                    elif k == NH + 2:
                        front(9)
                        pe.wait_ge(otlo_out, l * 4 + 1)
                        pe.wait_ge(vf_out, l * NB + NB)
                    elif k == NH + 3:
                        pe.wait_ge(o_out, l * 4 + 2)
                    elif k == NH + 6:
                        back(9)
                        pe.wait_ge(otlo_out, l * 4 + 2)
                    elif k == NH + 8:
                        front(10)
                    if k >= NH + 2:
                        u, b = divmod(k - (NH + 2), NB)
                        project(u, 1 - b, (9 + u // 3) % 2, u % 3 * UNIT)
                    if 1 <= k <= 2 * NH:
                        if k >= 2:
                            pe.wait_ge(prT_out, l * 2 * NH + (k - 1))
                        turn(k - 1, 7 if k <= NH else 5)
                    if k >= 2:
                        attend(k - 2, 0 if k - 2 < NH else 6)
                    if k == 7:
                        turn_outputs(0, 0)
                    if k == NH + 2:
                        turn_outputs(1, 7)
                    if k == NH + 7:
                        turn_outputs(2, 6)
                for u in range(4, KT):
                    if u == 4:
                        pe.wait_ge(otlo_out, l * 4 + 3)
                    if u == 5:
                        turn_outputs(3, 7)
                        back(10)
                    if u == 6:
                        pe.wait_ge(otlo_out, l * 4 + 4)
                        front(11)
                    if u == 7:
                        back(11)
                    for b in range(NB):
                        project(u, b, (9 + u // 3) % 2, u % 3 * UNIT if u < 7 else FRONT)

            for h in range(NH):
                pe.wait_ge(rb_set, 3 if h < NH // 2 else 4)
                if h >= 4:
                    pe.wait_ge(tab_sb, h - 3)
                nc.tensor.matmul(ps[:, h % 4, 0:TAB], rbhi[:, h, :], onehot_r, start=True, stop=False)
                nc.tensor.matmul(ps[:, h % 4, 0:TAB], rblo[:, h, :], onehot_r, start=False, stop=True).then_inc(tab_mm, 1)
            pe.wait_ge(ones_set, 1)
            with pe.Fori(0, DEPTH) as l:
                norm(l * 3)
                ffn(l, 0)
                norm(l * 3 + 1)
                mix(l)
                norm(l * 3 + 2)
                ffn(l, 1)

        @block.vector
        def _(dve):
            def split_front(l, k, i=0, used=FRONT, halves=(0, 1)):
                for half in halves:
                    s, at = k % 2, slice(half * (used // 2), (half + 1) * (used // 2))
                    dve.wait_ge(hi_front, chunk(l, k, i) * 2 + (half + 1))
                    nc.vector.tensor_tensor(wlo[:, s, at], raw[:, s, at], whi[:, s, at].bitcast(F32),
                                            ALU.subtract).then_inc(w_front, 1)

            def split_back(l, k, i=0, used=UNIT):
                s, at = k % 2, slice(FRONT, FRONT + used)
                dve.wait_ge(hi_back, chunk(l, k, i) + 1)
                nc.vector.tensor_tensor(wlo[:, s, at], raw[:, s, at], whi[:, s, at].bitcast(F32),
                                        ALU.subtract).then_inc(w_back, 1)

            def wait_apart(sem_, value, column=0):
                dve.wait_ge(sem_, value)
                nc.vector.memset(spare[:, column:column + 1], 0.0)

            def mean(n, b):
                dve.wait_ge(ss_out, n * NB + b + 1)
                nc.vector.tensor_scalar(ms[:, b:b + 1], ss[:, b:b + 1], 1.0 / D, EPS, ALU.mult, ALU.add
                                        ).then_inc(ms_out, 1)

            def norm(n, g, l, k, first=False):
                for t in range(KT):
                    if t % 2 == 0:
                        dve.wait_ge(xhi_out, n * KT + (t + 2))
                    nc.vector.scalar_tensor_tensor(
                        out=xlo[:, t, :], in0=ps[:, 4 + t // 2, S * (t % 2):S * (t % 2) + S],
                        scalar=gain[:, g + t:g + t + 1], in1=xhi[:, t, :].bitcast(F32),
                        op0=ALU.mult, op1=ALU.subtract).then_inc(xlo_out, 1)
                mean(n, 0)
                split_front(l, k, halves=(0,))
                mean(n, 1)
                for b in range(NB):
                    dve.wait_ge(rstd_out, n * NB + b + 1)
                    t = nc.vector.tensor_scalar(diag[:, b, :], ident, rstd[:, b:b + 1], None, ALU.mult)
                t.then_inc(diag_out, 1)
                split_front(l, k, halves=(1,))
                if first:
                    split_back(l, 0)
                dve.wait_ge(rows_mm, n + 1)
                nc.vector.tensor_copy(rows[:, :], ps[:, ROWS, 0:S]).then_inc(rows_out, 1)
                dve.wait_ge(rows_out, n + 1)

            def residual(b, j, factor):
                at = slice(j * 512, (j + 1) * 512)
                nc.vector.scalar_tensor_tensor(out=X[:, b, at], in0=ps[:, 2 * b + j, :], scalar=factor,
                                               in1=X[:, b, at], op0=ALU.mult, op1=ALU.add).then_inc(x_ready, 1)

            def ffn(l, phase):
                k0 = phase * (NF + MIXC)

                def step(f, i=0, back=UNIT, front=FRONT):
                    s, n = f % 2, l * (2 * NF) + i * 2 + (phase * NF + f)
                    gate, up = ((ps[:, 0, 0:S], ps[:, 1, 0:S]) if f == 0 else
                                (ps[:, GU + s, 0:S], ps[:, GU + s, S:2 * S]))
                    if f == NF - 1:
                        up = ps[:, LASTUP, 0:S]
                        dve.wait_ge(gate_mm, l * 2 + phase + 1)
                    else:
                        dve.wait_ge(front_done, n + 1)
                    nc.vector.tensor_tensor(hg[:, s, :], gate, rows[:, :], ALU.mult).then_inc(hg_out, 1)
                    if f < NF - 1:
                        nc.vector.tensor_tensor(ur[:, s, :], up, rows[:, :], ALU.mult).then_inc(ur_out, 1)
                    dve.wait_ge(sig_out, n + 1)
                    nc.vector.tensor_tensor(ht[:, s, :], hg[:, s, :], sig[:, s, :], ALU.mult).then_inc(ht_out, 1)
                    if f == NF - 1:
                        dve.wait_ge(front_done, n + 1)
                        nc.vector.tensor_tensor(ur[:, s, :], up, rows[:, :], ALU.mult).then_inc(ur_out, 1)
                    dve.wait_ge(ht_out, n + 1)
                    dve.wait_ge(ur_out, n + 1)
                    nc.vector.tensor_tensor(hf[:, s, :], ht[:, s, :], ur[:, s, :], ALU.mult).then_inc(h_out, 1)
                    dve.wait_ge(hhi_out, n + 1)
                    nc.vector.tensor_tensor(hlo[:, s, :], hf[:, s, :], hhi[:, s, :].bitcast(F32), ALU.subtract
                                            ).then_inc(hlo_out, 1)
                    if back:
                        split_back(l, k0 + f + 1, i, back)
                    if front:
                        split_front(l, k0 + f + 2, i, front)

                step(0)
                step(1)
                with dve.Fori(0, NF // 2 - 2) as i:
                    step(2, i)
                    step(3, i)
                step(NF - 2, front=MIX_USED[0][0] if phase == 0 else 0)
                step(NF - 1, back=MIX_USED[0][1] if phase == 0 else 0, front=0)
                dve.wait_ge(acc_mm, l * 5 + (3 * phase + 1))
                residual(0, 0, 0.5)
                residual(0, 1, 0.5)
                dve.wait_ge(acc_mm, l * 5 + (3 * phase + 2))
                residual(1, 0, 0.5)
                dve.wait_ge(back_done, l * (2 * NF) + (phase + 1) * NF)
                residual(1, 1, 0.5)

            def mix(l):
                def front(m, halves=(0, 1)):
                    split_front(l, NF + m, used=MIX_USED[m][0] if m < MIXC else FRONT, halves=halves)

                def back(m):
                    split_back(l, NF + m, used=MIX_USED[m][1] if m < MIXC else UNIT)

                def take(r0, r1):
                    ats = slice(0, P), slice(P, S3)
                    for r in range(r0, r1):
                        n = l * (2 * NB * (TOPK // 8)) + 2 * NB * r
                        for b in range(NB):
                            if r:
                                wait_apart(top_step, n - NB + (b + 1), b)
                            elif b == 0:
                                wait_apart(score_out, l * NH + NH)
                            nc.vector.max(top8[:, b, :], score[:, ats[b]]).then_inc(top_step, 1)
                        for b in range(NB):
                            wait_apart(top_step, n + (b + 1), NB + b)
                            nc.vector.match_replace(score[:, ats[b]], top8[:, b, :], score[:, ats[b]], TAKEN
                                                    ).then_inc(top_step, 1)

                def maxima(hh, bank):
                    g, h = divmod(hh, NH)
                    s = hh % 2
                    wait_apart(qk_mm, l * 2 * NH + (hh + 1))
                    for b, at, n in ((0, slice(0, P), P), (1, slice(P, S3), S)):
                        add = (bias[:, h, S - n:S] if g == 0 else cmask[:, S - n:S])
                        t = nc.vector.tensor_tensor_reduce(lg[:, s, at], ps[:, bank, at], add, 1.0, LOWEST,
                                                           ALU.add, ALU.max, mx[:, s, b:b + 1])
                    t.then_inc(lg_out, 1)
                    dve.wait_ge(lg_out, l * 2 * NH + (hh + 1))
                    if g == 0:
                        nc.vector.tensor_scalar(nm[:, s, :], mx[:, s, :], -SCALE, None, ALU.mult).then_inc(nm_out, 1)
                    else:
                        nc.vector.scalar_tensor_tensor(out=mt[:, s, :], in0=mx[:, s, :], scalar=SCALE,
                                                       in1=cumq[:, :, h], op0=ALU.mult, op1=ALU.add).then_inc(mt_out, 1)
                        dve.wait_ge(mt_out, l * NH + (h + 1))
                        nc.vector.tensor_tensor(nm[:, s, :], cumq[:, :, h], mt[:, s, :], ALU.subtract).then_inc(nm_out, 1)

                def turned(hh, bank):
                    dve.wait_ge(tr_mm, l * 2 * NH + (hh + 1))
                    nc.vector.tensor_copy(prT[:, hh % 2, :], ps[:, bank, 0:S3]).then_inc(prT_out, 1)

                def outputs(t, bank):
                    heads, g, half = slice(4 * t, 4 * t + 4), t // 2, t % 2
                    dve.wait_ge(pv_mm, l * 2 * NH + 4 * (t + 1))
                    nc.vector.reciprocal(rinv[:, :, heads], rsum[:, :, heads]).then_inc(rinv_out, 1)
                    dve.wait_ge(rinv_out, l * 4 + (t + 1))
                    for b in range(NB):
                        v = nc.vector.tensor_tensor(
                            xn[:, b, t * S:(t + 1) * S].rearrange("p (h d) -> p h d", h=4),
                            ps[:, bank, b * S:(b + 1) * S].rearrange("p (h d) -> p h d", h=4),
                            rinv[:, b, heads].unsqueeze(2).to_broadcast([P, 4, HD]), ALU.mult)
                    v.then_inc(o_out, 1)

                def out_low(t, bank):
                    dve.wait_ge(othi_out, l * 4 + (t + 1))
                    at = slice(2 * t, 2 * t + 2)
                    nc.vector.tensor_tensor(xlo[:, at, :].rearrange("p a t -> p (a t)"), ps[:, bank, :],
                                            xhi[:, at, :].rearrange("p a t -> p (a t)").bitcast(F32),
                                            ALU.subtract).then_inc(otlo_out, 1)

                def tile_out(j):
                    dve.wait_ge(feat_mm, l * NFEAT + j + 1)
                    nc.vector.tensor_tensor(feat[:, j, :], ps[:, GU + j % 2, 0:S], rows[:, :], ALU.mult
                                            ).then_inc(feat_out, 1)

                dve.wait_ge(table_out, 16)
                dve.wait_ge(const_in, 16)
                dve.wait_ge(c_mm, l + 1)
                nc.vector.tensor_tensor(ct, ps[:, CB, 0:S], rows[:, :], ALU.mult).then_inc(ct_out, 1)
                dve.wait_ge(feat_mm, l * NFEAT + KI + 1)
                nc.vector.tensor_copy(wft[:, :], ps[HD:KW, KIB, 0:S]).then_inc(wft_out, 1)
                for half in (slice(0, HD), slice(HD, P)):
                    t = nc.vector.tensor_tensor(feat[half, KI, :], ps[0:HD, KIB, 0:S], rows[0:HD, :], ALU.mult)
                t.then_inc(feat_out, 1)
                back(1)
                dve.wait_ge(wf_mm, l + 1)
                for b in range(NB):
                    at = b * 2 * NH
                    nc.vector.tensor_scalar(wf[:, b, :], ps[:, WFB, at:at + NH], rstd[:, b:b + 1],
                                            rstd[:, b:b + 1], ALU.mult, ALU.mult)
                    t = nc.vector.scalar_tensor_tensor(out=zf[:, b, :], in0=ps[:, WFB, at + NH:at + 2 * NH],
                                                       scalar=rstd[:, b:b + 1], in1=gain[:, G_BF:G_BF + NH],
                                                       op0=ALU.mult, op1=ALU.add)
                t.then_inc(z_out, 1)
                dve.wait_ge(z_out, l + 1)
                nc.vector.tensor_scalar(mz[:], zf[:], 0.0, None, ALU.min)
                nc.vector.scalar_tensor_tensor(out=az[:], in0=zf[:], scalar=-1.0, in1=zf[:], op0=ALU.mult,
                                               op1=ALU.max).then_inc(az_out, 1)
                dve.wait_ge(css_mm, l + 1)
                nc.vector.tensor_scalar(cms[:, :], ps[:, CB, 0:NB], 1.0 / P, EPS, ALU.mult, ALU.add).then_inc(cms_out, 1)
                dve.wait_ge(crstd_out, l + 1)
                for b in range(NB):
                    t = nc.vector.tensor_scalar(diag[:, b, :], ident, crstd[:, b:b + 1], None, ALU.mult)
                t.then_inc(cdiag_out, 1)
                dve.wait_ge(lz_out, l + 1)
                nc.vector.tensor_tensor(logf[:], mz[:], lz[:], ALU.subtract).then_inc(logf_out, 1)
                dve.wait_ge(crows_mm, l + 1)
                nc.vector.tensor_tensor(cn, ct, ps[:, CB, 0:S], ALU.mult).then_inc(cn_out, 1)
                front(2, (0,))
                front(2, (1,))
                back(2)
                dve.wait_ge(nc2_set, 1)
                dve.wait_ge(nchi_out, l + 1)
                for at, n in ((0, P), (P, S)):
                    t = nc.vector.scalar_tensor_tensor(
                        out=nc2[LO:LO + NH, at:at + n], in0=ps[0:NH, SUM, 0:n], scalar=-1.0 / SCALE,
                        in1=nc2[0:NH, at:at + n].bitcast(F32), op0=ALU.mult, op1=ALU.subtract)
                t.then_inc(nclo_out, 1)
                nc.vector.tensor_copy(cumq[:].rearrange("p b h -> p (b h)"),
                                      ps[:, SUM, CUMQ:CUMQ + NB * NH]).then_inc(cum_out, 1)
                dve.wait_ge(chi_out, l + 1)
                nc.vector.scalar_tensor_tensor(out=clo[:], in0=cn, scalar=gain[:, G_CKV:G_CKV + 1],
                                               in1=chi[:].bitcast(F32), op0=ALU.mult, op1=ALU.subtract
                                               ).then_inc(clo_out, 1)
                front(3)
                for h in range(NH):
                    dve.wait_ge(relu_out, l * NH + (h + 1))
                    if h:
                        dve.wait_ge(score_out, l * NH + h)
                    for b, at, n in ((0, slice(0, P), P), (1, slice(P, S3), S)):
                        t = nc.vector.scalar_tensor_tensor(
                            out=score[:, at], in0=relu[:, h % 2, at], scalar=wf[:, b, h:h + 1],
                            in1=score[:, at] if h else cmask[:, S - n:S], op0=ALU.mult, op1=ALU.add)
                    t.then_inc(score_out, 1)
                take(0, 1)
                tile_out(QA)
                take(1, 2)
                back(3)
                take(2, 3)
                tile_out(QA + 1)
                front(4, (0,))
                take(3, 4)
                tile_out(QA + 2)
                front(4, (1,))
                take(4, 5)
                back(4)
                tile_out(QA + 3)
                take(5, 6)
                front(5, (0,))
                tile_out(FX)
                take(6, 7)
                front(5, (1,))
                tile_out(FX + 1)
                take(7, 8)
                wait_apart(top_step, (l + 1) * (2 * NB * (TOPK // 8)))
                nc.vector.scalar_tensor_tensor(out=drop[:], in0=score[:], scalar=TAKEN, in1=noncausal,
                                               op0=ALU.not_equal, op1=ALU.max).then_inc(drop_out, 1)
                back(5)
                tile_out(FX + 2)
                front(6, (0,))
                front(6, (1,))
                tile_out(FX + 3)
                back(6)
                dve.wait_ge(bias_in, 16)
                for k in range(2 * NH + 2):
                    if k < 2 * NH:
                        maxima(k, 6 if k < NH else 4)
                    if k < 4:
                        tile_out(FX + 4 + k)
                    if 1 <= k <= 2 * NH:
                        turned(k - 1, 7 if k <= NH else 5)
                    if k == 1:
                        front(7)
                    if k == 2:
                        back(7)
                    if k == 4:
                        front(8)
                        back(8)
                    if k == 6:
                        front(9)
                        outputs(0, 0)
                    if k == 7:
                        back(9)
                    if k == NH + 1:
                        out_low(0, 0)
                        outputs(1, 1)
                    if k == NH + 2:
                        front(10)
                    if k == NH + 3:
                        back(10)
                    if k == NH + 3:
                        out_low(1, 7)
                    if k == NH + 6:
                        outputs(2, 6)
                        front(11)
                    if k == NH + 8:
                        out_low(2, 6)
                        back(11)
                outputs(3, 7)
                out_low(3, 7)
                front(12)
                back(12)
                dve.wait_ge(wo_mm, l * 2 * KT + (2 * KT - 1))
                residual(0, 0, 1.0)
                residual(0, 1, 1.0)
                dve.wait_ge(acc_mm, l * 5 + 3)
                residual(1, 0, 1.0)
                dve.wait_ge(wo_mm, l * 2 * KT + 2 * KT)
                residual(1, 1, 1.0)

            nc.vector.memset(ones[:], 1.0).then_inc(ones_set, 1)
            nc.vector.memset(nc2[:].bitcast(F32), 0.0).then_inc(nc2_set, 1)
            dve.wait_ge(rb_in, 16)
            dve.wait_ge(table_in, 16)
            rb_wide = rb.unsqueeze(2).to_broadcast([NBUCKET, NH, P])
            nc.vector.tensor_copy(rbhi, rb_wide).then_inc(rb_set, 1)
            nc.vector.tensor_copy(onehot_r, onehot).then_inc(rb_set, 1)
            dve.wait_ge(rb_set, 1)
            for half in (slice(0, NH // 2), slice(NH // 2, NH)):
                nc.vector.tensor_tensor(rblo[:, half, :], rb_wide[:, half, :], rbhi[:, half, :].bitcast(F32),
                                        ALU.subtract).then_inc(rb_set, 1)
            nc.vector.tensor_scalar(nident[:], ident, NEG, None, ALU.mult).then_inc(nident_set, 1)
            for b in range(NB):
                dve.wait_ge(x_in[b], 16)
                nc.vector.memset(spare[:, b:b + 1], 0.0).then_inc(x_ready, 2)
            with dve.Fori(0, DEPTH) as l:
                split_front(l, 0)
                norm(l * 3, G_FFN1, l, 1, first=True)
                ffn(l, 0)
                norm(l * 3 + 1, G_MIX, l, NF + 1)
                mix(l)
                norm(l * 3 + 2, G_FFN2, l, NF + MIXC + 1)
                ffn(l, 1)
            def close(b, j):
                at = slice(j * 512, (j + 1) * 512)
                nc.vector.scalar_tensor_tensor(out=xn[:, b, at], in0=X[:, b, at], scalar=rstd[:, b:b + 1],
                                               in1=fgain[:, at], op0=ALU.mult, op1=ALU.mult).then_inc(fin_out, 1)

            mean(DEPTH * 3, 0)
            dve.wait_ge(fgain_in, 16)
            dve.wait_ge(rstd_out, DEPTH * 3 * NB + 1)
            close(0, 0)
            mean(DEPTH * 3, 1)
            close(0, 1)
            dve.wait_ge(rstd_out, DEPTH * 3 * NB + 2)
            close(1, 0)
            close(1, 1)


def bucket(dist):
    dist, exact = max(dist, 0), NBUCKET // 2
    if dist < exact:
        return dist
    ratio = MAXDIST // exact
    steps = sum(dist ** exact >= exact ** exact * ratio ** k for k in range(1, exact + 1))
    return min(exact + steps, NBUCKET - 1)


def shape_constants():
    c = np.zeros((P, NC), np.float32)
    row, col = np.arange(P)[:, None], np.arange(P)[None, :]
    c[:, C_ID:C_ID + P] = row == col
    c[:, C_CM + P:C_CM + S] = np.where(col > row, np.float32(NEG), np.float32(0))
    c[:, C_NC:C_NC + P] = c[:, C_NC + 2 * P:C_NC + S3] = col > row
    for b in range(NB):
        c[:, C_U + b * S:C_U + (b + 1) * S] = b * P + row <= np.arange(S)[None, :]
    for h in range(NH):
        c[[h, LO + h], C_E + h * P:C_E + (h + 1) * P] = 1
    for y in range(TAB):
        c[bucket(2 * P - 1 - y), C_OH + y] = 1
    return c


def by_k(w, n):
    layers, k, cols = w.shape
    return w.reshape(layers, k // P, P, cols // n, n).transpose(0, 3, 2, 1, 4).reshape(layers, cols // n, P, -1)


def lay_out(a):
    f = np.float32
    stream = np.zeros((DEPTH, LC, P, CHUNK), f)
    for name, at in (("ffn1", 0), ("ffn2", NF + MIXC)):
        stream[:, at:at + NF, :, 0:UNIT] = by_k(a[name + "_gate"], P)
        stream[:, at:at + NF, :, UNIT:FRONT] = by_k(a[name + "_up"], P)
        stream[:, at:at + NF, :, FRONT:] = a[name + "_down"].reshape(DEPTH, NF, P, D)
    w = a["w_in"]
    hw = NH * HD
    at = np.cumsum([0, hw, P, NH * HD, HD, NH, hw, hw, hw, NH])
    qa, c, qi, ki, wi, fq, fk, fv, fl = (w[:, :, at[i]:at[i + 1]] for i in range(9))
    qa, qi, fq, fk = (by_k(t, P) for t in (qa, qi, fq, fk))
    fv = by_k(fv, hw)[:, 0]
    wo = a["w_out"].reshape(DEPTH, KT, P, D)
    place = {
        0: [np.concatenate([by_k(c, P)[:, 0], by_k(np.concatenate([ki, wi, fl], 2), KW)[:, 0]], 2)],
        1: [qi[:, 0], qi[:, 1], qi[:, 2]],
        2: [qi[:, 3], np.concatenate([a["w_uk"].reshape(DEPTH, P, hw), a["w_uv"].reshape(DEPTH, P, hw)], 2), qa[:, 0]],
        3: [qa[:, 1], qa[:, 2], qa[:, 3]],
        4: [fq[:, 0], fk[:, 0], fq[:, 1]],
        5: [fk[:, 1], fq[:, 2], fk[:, 2]],
        6: [fq[:, 3], fk[:, 3]],
        7: [fv[:, :, i * UNIT:(i + 1) * UNIT] for i in range(3)],
        8: [fv[:, :, 3 * UNIT:]],
        9: [wo[:, 0], wo[:, 1], wo[:, 2]],
        10: [wo[:, 3], wo[:, 4], wo[:, 5]],
        11: [wo[:, 6], None, wo[:, 7]],
    }
    for m, parts in place.items():
        for i, part in enumerate(parts):
            if part is not None:
                stream[:, NF + m, :, i * UNIT:i * UNIT + part.shape[2]] = part
    gains = np.zeros((P, DEPTH, NG), f)
    for name, col in (("ffn1_norm", G_FFN1), ("mix_norm", G_MIX), ("ffn2_norm", G_FFN2)):
        gains[:, :, col:col + KT] = a[name].reshape(DEPTH, KT, P).transpose(2, 0, 1)
    gains[:, :, G_CKV] = a["ckv_norm"].T
    gains[:, :, G_BF:] = a["b_forget"][None]
    return {
        "x": np.ascontiguousarray(a["x"].reshape(NB, P, D).transpose(1, 0, 2)),
        "stream": stream.reshape(NCHUNK, P, CHUNK),
        "gains": gains,
        "final_gain": np.ascontiguousarray(np.broadcast_to(a["final_norm"][None], (P, D))),
        "consts": shape_constants(),
        "rel_bias": np.ascontiguousarray(a["rel_bias"]),
    }


def kernel(**inputs):
    import concourse.bacc as bacc
    from concourse.bass_utils import run_bass_kernel_spmd

    arrays = lay_out({k: np.asarray(v) for k, v in inputs.items()})
    nc = bacc.Bacc("TRN2", target_bir_lowering=False, num_devices=1)
    args = [nc.dram_tensor(k, v.shape, F32, kind="ExternalInput").ap() for k, v in arrays.items()]
    out = nc.dram_tensor("out", (NB, P, D), F32, kind="ExternalOutput").ap()
    table = nc.dram_tensor("table", (NH, P * TAB), F32, kind="Internal").ap()
    trunk(nc, *args, out, table)
    r = run_bass_kernel_spmd(nc, [arrays], core_ids=[0])
    return r.results[0]["out"].reshape(1, S, D)
```
